# Optimizing a Trainium2 kernel written in Bass

```python
import math
import jax, jax.numpy as jnp
from jax import lax
import numpy as np

D_MODEL = 2048
BATCH = 1
SEQ = 256
DEPTH = 1

HEAD_DIM = 64
N_Q_HEADS = 16
N_KV_HEADS = 4
Q_PER_KV = N_Q_HEADS // N_KV_HEADS
ATTN_WIDTH = N_Q_HEADS * HEAD_DIM
KV_WIDTH = N_KV_HEADS * HEAD_DIM
WINDOW = 128
BLOCK = 128
NUM_BUCKETS = 32
MAX_EXACT = NUM_BUCKETS // 2
MAX_DISTANCE = 128
CONV_CHANNELS = D_MODEL // 2
CONV_WIDTH = 31
D_FF = ((8 * D_MODEL + 3 * 256 - 1) // (3 * 256)) * 256
EPS = 1e-6
IN_SIZES = [ATTN_WIDTH, KV_WIDTH, KV_WIDTH, CONV_CHANNELS, CONV_CHANNELS, D_MODEL, D_MODEL]
IN_WIDTH = sum(IN_SIZES)
IN_SPLITS = [int(s) for s in np.cumsum(IN_SIZES)[:-1]]
N_MOD = 6

kernel_name = "hybrid_swa_sink_conformer_conv_gated_block"

def rms_norm(x, g):
    xf = x.astype(jnp.float32)
    y = xf * lax.rsqrt(jnp.mean(xf * xf, axis=-1, keepdims=True) + EPS)
    return (y * g.astype(jnp.float32)).astype(x.dtype)

def layer_norm(x, g, b):
    xf = x.astype(jnp.float32)
    mu = jnp.mean(xf, axis=-1, keepdims=True)
    var = jnp.mean(jnp.square(xf - mu), axis=-1, keepdims=True)
    y = (xf - mu) * lax.rsqrt(var + EPS)
    return (y * g.astype(jnp.float32) + b.astype(jnp.float32)).astype(x.dtype)

def t5_causal_bucket(dist):
    n = jnp.maximum(dist, 0)
    nf = jnp.maximum(n, 1).astype(jnp.float32)
    large = MAX_EXACT + (jnp.log(nf / MAX_EXACT) / math.log(MAX_DISTANCE / MAX_EXACT)
                         * (NUM_BUCKETS - MAX_EXACT)).astype(jnp.int32)
    large = jnp.minimum(large, NUM_BUCKETS - 1)
    return jnp.where(n < MAX_EXACT, n, large)

def sliding_window_attention(q, k, v, rel_bias, sinks, q_g, k_g):
    b_sz, s_len = q.shape[0], q.shape[1]
    nb = s_len // BLOCK
    q = rms_norm(q, q_g)
    k = rms_norm(k, k_g)
    qb = q.reshape(b_sz, nb, BLOCK, N_KV_HEADS, Q_PER_KV, HEAD_DIM)

    def band(t):
        tb = t.reshape(b_sz, nb, BLOCK, N_KV_HEADS, HEAD_DIM)
        prev = jnp.concatenate([jnp.zeros_like(tb[:, :1]), tb[:, :-1]], axis=1)
        return jnp.concatenate([prev, tb], axis=2)

    kw, vw = band(k), band(v)
    logits = jnp.einsum('bnqhgd,bnkhd->bnhgqk', qb, kw).astype(jnp.float32) * (HEAD_DIM ** -0.5)

    q_off = jnp.arange(BLOCK)
    k_off = jnp.arange(2 * BLOCK)
    dist = q_off[:, None] + BLOCK - k_off[None, :]
    bias = rel_bias.astype(jnp.float32)[t5_causal_bucket(dist)]
    bias = jnp.transpose(bias, (2, 0, 1)).reshape(N_KV_HEADS, Q_PER_KV, BLOCK, 2 * BLOCK)
    allowed = (dist >= 0) & (dist < WINDOW)
    real_key = (jnp.arange(nb)[:, None, None] > 0) | (k_off[None, None, :] >= BLOCK)
    mask = allowed[None] & real_key

    logits = jnp.where(mask[None, :, None, None], logits + bias, -jnp.inf)
    sink = sinks.astype(jnp.float32).reshape(N_KV_HEADS, Q_PER_KV)[None, None, :, :, None, None]
    m = jnp.maximum(jnp.max(logits, axis=-1, keepdims=True), sink)
    p = jnp.exp(logits - m)
    probs = p / (jnp.sum(p, axis=-1, keepdims=True) + jnp.exp(sink - m))
    out = jnp.einsum('bnhgqk,bnkhd->bnqhgd', probs.astype(v.dtype), vw)
    return out.reshape(b_sz, s_len, ATTN_WIDTH)

def conformer_conv(a, gate, conv_w, conv_b, ln_g, ln_b, w_out):
    u = a * jax.nn.sigmoid(gate)
    u = lax.conv_general_dilated(
        u, conv_w[:, None, :].astype(u.dtype), window_strides=(1,),
        padding=[(CONV_WIDTH - 1, 0)], dimension_numbers=('NWC', 'WIO', 'NWC'),
        feature_group_count=CONV_CHANNELS) + conv_b
    u = jax.nn.silu(layer_norm(u, ln_g, ln_b))
    return u @ w_out

def setup_inputs(seed: int = 0) -> dict:
    key = jax.random.key(seed)
    ks = jax.random.split(key, 24)
    nrm = lambda k, shape, s: jax.random.normal(k, shape, jnp.float32) * s
    d = D_MODEL
    return {
        "x": nrm(ks[0], (BATCH, SEQ, d), 1.0),
        "c": nrm(ks[1], (BATCH, d), 1.0),
        "w_ada": nrm(ks[2], (DEPTH, d, N_MOD * d), 0.5 * d ** -0.5),
        "b_ada": nrm(ks[3], (DEPTH, N_MOD * d), 0.02),
        "norm_mix_g": 1.0 + nrm(ks[4], (DEPTH, d), 0.02),
        "w_in": nrm(ks[5], (DEPTH, d, IN_WIDTH), d ** -0.5),
        "q_norm_g": 1.0 + nrm(ks[6], (DEPTH, HEAD_DIM), 0.02),
        "k_norm_g": 1.0 + nrm(ks[7], (DEPTH, HEAD_DIM), 0.02),
        "attn_sinks": nrm(ks[8], (DEPTH, N_Q_HEADS), 0.5),
        "rel_bias": nrm(ks[9], (NUM_BUCKETS, N_Q_HEADS), 0.5),
        "w_attn_out": nrm(ks[10], (DEPTH, ATTN_WIDTH, d), ATTN_WIDTH ** -0.5),
        "conv_w": nrm(ks[11], (DEPTH, CONV_WIDTH, CONV_CHANNELS), CONV_WIDTH ** -0.5),
        "conv_b": nrm(ks[12], (DEPTH, CONV_CHANNELS), 0.02),
        "conv_ln_g": 1.0 + nrm(ks[13], (DEPTH, CONV_CHANNELS), 0.02),
        "conv_ln_b": nrm(ks[14], (DEPTH, CONV_CHANNELS), 0.02),
        "w_conv_out": nrm(ks[15], (DEPTH, CONV_CHANNELS, d), CONV_CHANNELS ** -0.5),
        "w_mix_out": nrm(ks[16], (DEPTH, d, d), d ** -0.5),
        "norm_ffn_g": 1.0 + nrm(ks[17], (DEPTH, d), 0.02),
        "w_ffn_in": nrm(ks[18], (DEPTH, d, 2 * D_FF), d ** -0.5),
        "w_ffn_out": nrm(ks[19], (DEPTH, D_FF, d), D_FF ** -0.5),
    }

def reference(x, c, w_ada, b_ada, norm_mix_g, w_in, q_norm_g, k_norm_g, attn_sinks, rel_bias,
              w_attn_out, conv_w, conv_b, conv_ln_g, conv_ln_b, w_conv_out, w_mix_out,
              norm_ffn_g, w_ffn_in, w_ffn_out):
    b_sz, s_len = x.shape[0], x.shape[1]
    c_act = jax.nn.silu(c)
    for l in range(DEPTH):
        mod = (c_act @ w_ada[l] + b_ada[l])[:, None, :]
        sh_m, sc_m, gt_m, sh_f, sc_f, gt_f = jnp.split(mod, N_MOD, axis=-1)

        h = rms_norm(x, norm_mix_g[l]) * (1.0 + sc_m) + sh_m
        q, k, v, ca, cb, g_attn, g_conv = jnp.split(h @ w_in[l], IN_SPLITS, axis=-1)
        q = q.reshape(b_sz, s_len, N_Q_HEADS, HEAD_DIM)
        k = k.reshape(b_sz, s_len, N_KV_HEADS, HEAD_DIM)
        v = v.reshape(b_sz, s_len, N_KV_HEADS, HEAD_DIM)
        y_attn = sliding_window_attention(q, k, v, rel_bias, attn_sinks[l],
                                          q_norm_g[l], k_norm_g[l]) @ w_attn_out[l]
        y_conv = conformer_conv(ca, cb, conv_w[l], conv_b[l], conv_ln_g[l], conv_ln_b[l],
                                w_conv_out[l])
        merged = jax.nn.sigmoid(g_attn) * y_attn + jax.nn.sigmoid(g_conv) * y_conv
        x = x + gt_m * (merged @ w_mix_out[l])

        h = rms_norm(x, norm_ffn_g[l]) * (1.0 + sc_f) + sh_f
        f_gate, f_up = jnp.split(h @ w_ffn_in[l], 2, axis=-1)
        x = x + gt_f * ((jax.nn.silu(f_gate) * f_up) @ w_ffn_out[l])
    return x


_drawn_inputs = setup_inputs


def setup_inputs(seed=0):
    import zlib

    import numpy as np

    out = dict(_drawn_inputs(seed))
    spreads = {}
    factors = {'b_ada': 2.994,
     'norm_mix_g': 8.0,
     'q_norm_g': 8.0,
     'k_norm_g': 8.0,
     'attn_sinks': 139.947,
     'rel_bias': 3.959,
     'conv_b': 8.0,
     'conv_ln_g': 29.52,
     'conv_ln_b': 30.882,
     'norm_ffn_g': 8.0}
    for name, (base, spread) in spreads.items():
        noise = np.random.default_rng([zlib.crc32(name.encode()), seed]).standard_normal(out[name].shape)
        drawn = base * np.exp(spread * noise) if base else spread * noise
        out[name] = __import__('jax').numpy.asarray(drawn.astype(out[name].dtype))
    for name, factor in factors.items():
        out[name] = (out[name] * factor).astype(out[name].dtype)
    return out
```

```python
from contextlib import ExitStack

import concourse.bass as bass
from concourse import mybir

f32 = mybir.dt.float32
f32r = mybir.dt.float32r
ALU = mybir.AluOpType
ACT = mybir.ActivationFunctionType

P = 128
D = 2048
TOK = 256
HEAD = 64
HEADS = 16
KV = 4
CONV_W = 31
CONV_C = D // 2
DFF = 5632
EPS = 1e-6
MASKED = -1.0e30
COLS = 512
GT = COLS // P
UK = 2
KT = D // P
AT_T = HEADS * HEAD // P
CT_T = CONV_C // P
FT = DFF // P
RING = 4
LEAD = 3
U_D = KT // UK
U_H = AT_T // UK
U_F = FT // UK
Q0, K0, V0, CA0, CB0, GA0, GC0 = 0, 8, 10, 12, 20, 28, 44
Z_T = 60
N_PROJ = 7
N_GATE = 8
LEAD_ADA = 8
WIDE = 2 * COLS
U_PROJ = 0
U_GATE = U_PROJ + N_PROJ * U_D
U_MERGE = U_GATE + N_GATE * U_D
U_MIX = U_MERGE + 4 * 2 * U_H
U_FIN = U_MIX + 4 * U_D
U_FOUT = U_FIN + 11 * 2 * U_D
U_END = U_FOUT + 4 * U_F
T_PROJ = 0
T_GATE = T_PROJ + N_PROJ * GT
T_MERGE = T_GATE + N_GATE * GT
T_MIX = T_MERGE + 4 * 2 * GT
T_FIN = T_MIX + 4 * GT
T_FOUT = T_FIN + 11 * 2 * GT
LEAD_U = LEAD_ADA // 2 * U_D
A_PROJ = LEAD_U
A_MERGE = A_PROJ + N_PROJ * U_D
A_MIX = A_MERGE + KT
A_FOUT = A_MIX + 4 * U_D
SMALL = 16
CLEARS = 6
TAPS = [3, 4, 3, 4, 4, 5, 4, 4]


class Steps:

    def __init__(self, eng, sem):
        self.eng, self.sem, self.n, self.round = eng, sem, 0, 0

    def step(self, ins):
        ins.then_inc(self.sem, 1)
        self.n += 1

    def wait(self):
        self.eng.wait_ge(self.sem, self.round + self.n)

    def each(self, rounds, per):
        at = self.n
        with self.eng.Fori(0, rounds) as i:
            self.round = i * per
            yield i
            assert self.n - at == per, f"{self.n - at} steps a round, not {per}"
        self.round = 0
        self.n = at + rounds * per


def hold(eng, sem, value, started):
    eng.wait_ge(started, 1)
    eng.wait_ge(sem, value)


def build(nc, x, c, w_ada, b_ada, norm_mix_g, w_in, q_norm_g, k_norm_g, attn_sinks, rel_bias,
          w_attn_out, conv_w, conv_b, conv_ln_g, conv_ln_b, w_conv_out, w_mix_out, norm_ffn_g,
          w_ffn_in, w_ffn_out, squares, onehot, out):
    toeplitz = nc.dram_tensor("toeplitz_rows", (HEADS, 3 * P), f32, kind="Internal")

    with ExitStack() as ctx:
        base = 1152
        at = {"free": base}

        def place(name, shape, dt=f32, offset=None):
            size = 4
            for s in shape[1:]:
                size *= s
            if offset is None:
                offset = at["free"]
                at["free"] += (size + 31) // 32 * 32
            return nc.alloc_sbuf_tensor_at(name, shape, dt, offset=offset)

        def sem(name):
            return ctx.enter_context(nc.semaphore(name))

        raw = [place(f"raw{s}", [P, UK, COLS]) for s in range(RING)]
        w_hi = [place(f"w_hi{s}", [P, UK, COLS], f32r) for s in range(RING)]
        lead_off = at["free"]
        w_lo = [place(f"w_lo{s}", [P, UK, COLS], f32r) for s in range(RING)]
        ada = [place(f"ada{s}", [P, UK, COLS]) for s in range(RING)]
        wide_ada = [place(f"wide_ada{s}", [P, UK, WIDE], offset=lead_off + s * UK * WIDE * 4) for s in range(RING)]
        hs_off = at["free"]
        hs = place("h_split", [P, KT, 2, TOK], f32r)
        xT = place("xT", [P, KT, TOK])
        sq4 = place("squares", [P, 4, P])
        ident, flip, swap, head_mean = (sq4[:, n, :] for n in range(4))
        ones = place("ones", [P, P])
        rowsT = place("rowsT", [P, 168])
        conv_wT = place("conv_wT", [P, CT_T, 32])
        mod = place("mod", [P, 96])
        gain = place("gain", [P, KT])
        acc = place("ada_acc", [P, COLS])
        low = [place(f"low{s}", [P, TOK]) for s in range(2)]
        vo = at["free"]
        val = [place(f"val{s}", [P, TOK]) for s in range(GT)]
        probT = place("probT", [P, 2, 3 * P], offset=vo)
        usum = place("sum_sq", [P, TOK])
        rstd = place("rstd", [P, TOK])
        qk_g = place("qk_gain", [P, 2])
        sinks = place("sinks", [P, HEADS])
        padded = place("conv_padded", [P, CONV_W - 1 + TOK])
        conv_acc = place("conv_acc", [P, TOK])
        taps_now = place("taps_now", [P, 32])
        v_now = place("v_now", [P, 2, 3 * HEAD])
        sink_now = place("sink_now", [P, 2])
        stats = place("softmax_stats", [P, 5, 4])
        s_max, s_neg, s_den, s_sink, s_rec = (stats[:, n, :] for n in range(5))
        uo = at["free"]
        q_now = place("q_now", [P, TOK])
        logit = place("logit", [P, 2, 3 * P])
        up = [place(f"up{s}", [P, TOK], offset=uo + s * TOK * 4) for s in range(GT)]
        wide_done = place("wide_acc_done", [P, WIDE], offset=uo)
        acc_done = wide_done[:, COLS:]
        eps = place("eps", [P, 1])
        zo = at["free"]
        z = place("z", [P, Z_T, TOK], offset=zo)
        attn = place("attn_split", [P, CB0 + CT_T, TOK], f32r, offset=zo)
        xn = place("xn", [P, KT, TOK], offset=zo + GA0 * TOK * 4)
        xtok = place("x_rows", [P, 2, D], offset=zo)
        bo = zo + Z_T * TOK * 4
        bias = place("bias", [P, HEADS, 2 * P], offset=bo)
        conv_sq = place("conv_sq", [P, CT_T, TOK], offset=bo)
        conv = place("conv_split", [P, CT_T, 2, TOK], f32r, offset=bo)
        ko = bo + 4 * HEADS * 2 * P
        kz = place("k_padded", [P, 2, KV, TOK], offset=ko)
        vt = place("v_rows", [P, 2, KV * HEAD], offset=ko + 8192)
        bias_now = place("bias_now", [P, 2, 2 * P], offset=ko + 10240)
        wide_acc = place("wide_acc", [P, WIDE], offset=zo + 50 * TOK * 4)
        hid = place("hidden_split", [P, FT, 2, TOK], f32r, offset=zo)
        end = zo + 4 * FT * 2 * TOK
        assert ko + 12288 <= end
        assert end <= 229344, end
        out_t = place("out_t", [P, GT, TOK], offset=hs_off)
        out_rows = [place(f"out_rows{s}", [P, 2, COLS], offset=hs_off + 4096 * (1 + s)) for s in range(4)]
        reversed_bias = place("reversed_bias", [P, HEADS, 2 * P], offset=hs_off)
        table = place("bias_table", [HEADS, 3 * P], offset=hs_off + 16384)
        rows1 = place("rows1", [112, P], offset=hs_off + 18432)
        rows2 = place("rows2", [56, P], offset=hs_off + 19456)
        taps_rows = place("taps_rows", [CONV_W, CONV_C], offset=hs_off + 20480)
        rel = place("rel", [32, HEADS], offset=hs_off + 24576)
        buckets = place("buckets", [32, P], offset=hs_off + 25600)
        xsq = place("x_sq", [P, KT, TOK], offset=bo)

        ps = [ctx.enter_context(nc.psum_tensor(f"ps{b}", [P, 512], f32)) for b in range(8)]

        c_col = rowsT[:, 0:16]
        b_ada_col = rowsT[:, 16:112]
        g_mix, g_ffn = rowsT[:, 112:128], rowsT[:, 128:144]
        cb_col, lg_col, lb_col = rowsT[:, 144:152], rowsT[:, 152:160], rowsT[:, 160:168]

        raw_here = [sem(f"raw_here{s}") for s in range(RING)]
        hi_ready = sem("hi_ready")
        w_split = sem("w_split")
        w_used = sem("w_used")
        ada_here = [sem(f"ada_here{s}") for s in range(RING)]
        ada_free = sem("ada_free")
        tile_done = sem("tile_done")
        low_ready = sem("low_ready")
        bank_free = sem("bank_free")
        act_self, dve_self, pool_self = sem("act_self"), sem("dve_self"), sem("pool_self")
        small_here, x_here, const_here = sem("small_here"), sem("x_here"), sem("const_here")
        rows_t, rows_out = sem("rows_transposed"), sem("rows_out")
        table_sum, table_ready, table_stored, bias_here = (
            sem("table_sum"), sem("table_ready"), sem("table_stored"), sem("bias_here"))
        flipped, bias_out = sem("flipped"), sem("bias_out")
        xt_done, xt_out = sem("xt_done"), sem("xt_out")
        cleared = sem("cleared")
        xsq_ready, sum_ready, ms_ready, root_ready = (
            sem("xsq_ready"), sem("sum_ready"), sem("ms_ready"), sem("root_ready"))
        mod_sum, c_ready, cleared2 = sem("mod_sum"), sem("c_ready"), sem("late_cleared")
        h_val, h_hi, h_ready = sem("h_val"), sem("h_hi"), sem("h_ready")
        z_out = sem("z_out")
        norm_sq, norm_ms, norm_root, k_ready = (
            sem("norm_sq"), sem("norm_ms"), sem("norm_root"), sem("k_ready"))
        swapped, k_padded, v_t, v_out, cb_sig = (
            sem("swapped"), sem("k_padded"), sem("v_t"), sem("v_out"), sem("cb_sig"))
        q_ready = sem("q_ready")
        now_ready, s_done, neg_ready, exp_ready, p_ready = (
            sem("now_ready"), sem("s_done"), sem("neg_ready"), sem("exp_ready"), sem("p_ready"))
        pt_done, pt_out, o_done, o_hi, o_out = (
            sem("pt_done"), sem("pt_out"), sem("o_done"), sem("o_hi"), sem("o_out"))
        conv_out, mean_sum, centered, csq_ready, var_sum, croot, cnorm, silu_ready, chi, conv_ready = (
            sem("conv_out"), sem("mean_sum"), sem("centered"), sem("csq_ready"), sem("var_sum"),
            sem("croot"), sem("cnorm"), sem("silu_ready"), sem("conv_hi"), sem("conv_ready"))
        gate_sig, m_val, m_hi, m_ready = sem("gate_sig"), sem("m_val"), sem("m_hi"), sem("m_ready")
        x2_ready, x2_sq = sem("x2_ready"), sem("x2_sq")
        sq_summed = sem("sq_summed")
        g_silu, f_val, f_hi, f_ready = sem("g_silu"), sem("f_val"), sem("f_hi"), sem("f_ready")
        o_val, o_t, rows_ready, stored = sem("o_val"), sem("o_t"), sem("rows_ready"), sem("stored")

        block = ctx.enter_context(nc.Block())

        @block.sync
        def _(sp):
            def weights(u, w, row, col):
                number, slot = u
                sp.wait_ge(w_split, number + 1)
                sp.dma_start(raw[slot][:, :, :],
                             w[row:row + UK * P, bass.ds(col, COLS)].rearrange("(a p) n -> p a n", p=P)
                             ).then_inc(raw_here[slot], 16)

            def ada_unit(number, slot, row, col):
                sp.wait_ge(ada_free, number + 1)
                sp.dma_start(ada[slot][:, :, :],
                             w_ada[bass.ds(row, UK * P), bass.ds(col, COLS)].rearrange("(a p) n -> p a n", p=P)
                             ).then_inc(ada_here[slot], 16)

            for half in range(2):
                with sp.Fori(0, 2) as n:
                    for k in range(U_D):
                        sp.wait_ge(ada_free, n * U_D + (half * LEAD_U // 2 + k + 1))
                        sp.dma_start(wide_ada[k % RING][:, :, :],
                                     w_ada[k * UK * P:(k + 1) * UK * P, bass.ds(n * D + half * WIDE, WIDE)]
                                     .rearrange("(a p) n -> p a n", p=P)).then_inc(ada_here[k % RING], 16)
            for k in range(LEAD):
                weights((U_PROJ + k, k), w_in, k * UK * P, 0)
            with sp.Fori(0, N_PROJ) as g:
                for k in range(U_D):
                    n = k + LEAD
                    weights((g * U_D + (U_PROJ + n), n % RING), w_in, n % U_D * UK * P, (g + n // U_D) * COLS)
                    if k == 0:
                        sp.wait_ge(ada_free, LEAD_U + RING)
                    ada_unit(g * U_D + (A_PROJ + k), k % RING, k * UK * P, g * COLS + LEAD_ADA * COLS)
            for k in range(LEAD, U_D):
                weights((U_GATE + k, k % RING), w_in, k * UK * P, N_PROJ * COLS)
            with sp.Fori(1, N_GATE) as g:
                for k in range(U_D):
                    weights((g * U_D + (U_GATE + k), k % RING), w_in, k * UK * P, g * COLS + N_PROJ * COLS)
            with sp.Fori(0, 4) as g:
                for n, w in enumerate((w_attn_out, w_conv_out)):
                    for k in range(U_H):
                        weights((g * (2 * U_H) + (U_MERGE + n * U_H + k), k % RING), w, k * UK * P, g * COLS)
                        if n == 0:
                            sp.wait_ge(ada_free, g * 4 + (A_MERGE + k + 1))
                            sp.dma_start(ada[k][:, 0, :],
                                         w_ada[bass.ds(g * (4 * P) + k * P, P), 15 * COLS:16 * COLS]
                                         ).then_inc(ada_here[k], 16)
            for k in range(LEAD):
                weights((U_MIX + k, k), w_mix_out, k * UK * P, 0)

            def mix_out(g, last):
                for k in range(U_D):
                    n = k + LEAD
                    if n < U_D or not last:
                        weights((g * U_D + (U_MIX + n), n % RING), w_mix_out, n % U_D * UK * P, (g + n // U_D) * COLS)
                    ada_unit(g * U_D + (A_MIX + k), k % RING, k * UK * P, (g + 16) * COLS)

            with sp.Fori(0, 3) as g:
                mix_out(g, False)
            mix_out(3, True)
            with sp.Fori(0, 11) as g:
                for n in range(2):
                    for k in range(U_D):
                        weights((g * (2 * U_D) + (U_FIN + n * U_D + k), k % RING), w_ffn_in,
                                k * UK * P, g * COLS + n * DFF)
            with sp.Fori(0, 2) as g:
                for h in range(2):
                    for k in range(U_F):
                        weights((g * (2 * U_F) + (U_FOUT + h * U_F + k), (h * U_F + k) % RING), w_ffn_out,
                                k * UK * P, g * (2 * COLS) + h * COLS)
                        a = k - LEAD
                        if 0 <= a < U_D:
                            ada_unit(g * (2 * U_D) + (A_FOUT + h * U_D + a), a % RING, a * UK * P,
                                     g * (2 * COLS) + (20 + h) * COLS)
            for g in range(4):
                sp.wait_ge(rows_ready, 2 * (g + 1))
                sp.dma_start(out[:, g * COLS:(g + 1) * COLS].rearrange("(b p) n -> p b n", p=P),
                             out_rows[g][:, :, :]).then_inc(stored, 16)
            sp.wait_ge(stored, 4 * 16)

        @block.gpsimd
        def _(pool):
            pool.memset(ones[:, :], 1.0).then_inc(cleared, 1)
            pool.memset(eps[:, :], EPS).then_inc(cleared, 1)
            pool.memset(table[:, :], MASKED).then_inc(cleared, 1)
            pool.memset(padded[:, :], 0.0).then_inc(cleared, 1)
            pool.memset(v_now[:, :, :], 0.0).then_inc(cleared, 1)
            pool.memset(kz[:, :, :, :], 0.0).then_inc(cleared, 1)

        @block.scalar
        def _(act):
            def split_high(number, slot, turn):
                act.wait_ge(raw_here[slot], turn)
                act.wait_ge(w_used, number + 1)
                act.activation(w_hi[slot][:, :, :], raw[slot][:, :, :], ACT.Copy).then_inc(hi_ready, 1)

            def ahead(first, k, i=0, per=0):
                n = first + k + LEAD
                if n < U_END:
                    split_high(i * per + n, n % RING, i * (per // RING * 16) + (n // RING + 1) * 16)

            def lows(tile, groups3, used):
                for t in range(GT):
                    if t < GT - 1:
                        act.wait_ge(tile_done, groups3 + (t + 1))
                    else:
                        act.wait_ge(w_used, used)
                    act.wait_ge(bank_free, tile + (t + 3))
                    act.activation(low[t % 2][:, :], ps[t][:, TOK:], ACT.Copy).then_inc(low_ready, 1)

            act.dma_start(sq4[:, :, :], squares).then_inc(small_here, 16)
            act.dma_start(rows1[0:16, :], c).then_inc(small_here, 16)
            act.dma_start(rows1[16:112, :], b_ada).then_inc(small_here, 16)
            for n, (v, m) in enumerate(((norm_mix_g, 16), (norm_ffn_g, 16), (conv_b, 8), (conv_ln_g, 8),
                                        (conv_ln_b, 8))):
                r = (0, 16, 32, 40, 48)[n]
                act.dma_start(rows2[r:r + m, :], v).then_inc(small_here, 16)
            act.dma_start(taps_rows[:, :], conv_w).then_inc(small_here, 16)
            act.dma_start(rel[:, :], rel_bias).then_inc(small_here, 16)
            act.dma_start(buckets[:, :], onehot).then_inc(small_here, 16)
            for n, v in enumerate((q_norm_g, k_norm_g)):
                for h in range(2):
                    act.dma_start(qk_g[h * HEAD:(h + 1) * HEAD, n:n + 1], v).then_inc(small_here, 16)
            act.dma_start(sinks[:, :], attn_sinks.broadcast_to([P, HEADS])).then_inc(small_here, 16)
            for b in range(2):
                act.dma_start(xtok[:, b, :], x[b * P:(b + 1) * P, :]).then_inc(x_here, 16)
            act.wait_ge(rows_out, 1)
            act.activation(c_col, c_col, ACT.Silu).then_inc(c_ready, 1)
            act.wait_ge(table_ready, 1)
            act.dma_start(toeplitz.ap(), table[:, :]).then_inc(table_stored, 16)
            act.wait_ge(table_stored, 16)
            shifted = bass.AP(toeplitz.ap().tensor, 0, [[1, P], [3 * P, HEADS], [1, 2 * P]])
            act.dma_start(reversed_bias[:, :, :], shifted).then_inc(bias_here, 16)
            for b in range(KT // 2):
                act.wait_ge(xt_done, b + 1)
                act.activation(xT[:, 2 * b:2 * b + 2, :], ps[b % 4][:, :], ACT.Copy)
                act.activation(xsq[:, 2 * b:2 * b + 2, :], ps[b % 4][:, :], ACT.Square).then_inc(xsq_ready, 1)
            act.wait_ge(sum_ready, 1)
            act.wait_ge(cleared, CLEARS)
            act.activation(rstd[:, :], ps[4][:, :TOK], ACT.Sqrt, bias=eps[:, :], scale=1.0 / D
                           ).then_inc(root_ready, 1)
            for b in range(HEADS // 2):
                act.wait_ge(flipped, b + 1)
                act.activation(bias[:, 2 * b:2 * b + 2, :], ps[5 + b % 2][:, :], ACT.Copy).then_inc(bias_out, 1)

            def high_h(first, t, shift):
                act.wait_ge(h_val, first + t + 1)
                act.activation(hs[:, t, 0, :], xn[:, t, :], ACT.Identity, bias=mod[:, shift + t:shift + t + 1]
                               ).then_inc(h_hi, 1)

            for t in range(KT // 2):
                high_h(0, t, 0)
            for n in range(LEAD):
                ahead(U_PROJ - LEAD, n)
            for t in range(KT // 2, KT):
                high_h(0, t, 0)
            with act.Fori(0, N_PROJ) as g:
                for k in range(U_D):
                    ahead(U_PROJ, k, g, U_D)
                lows(g * GT + T_PROJ, g * 3 + T_PROJ // GT * 3, g * U_D + (U_PROJ + U_D + RING))

            act.wait_ge(bank_free, T_GATE + GT)
            for n in range(5):
                act.activation(z[:, GA0 + 2 * n:GA0 + 2 * n + 2, :], z[:, 2 * n:2 * n + 2, :], ACT.Square
                               ).then_inc(norm_sq, 1)
            for n in range(5):
                act.wait_ge(norm_ms, n + 1)
                act.activation(z[:, GA0 + 10 + 2 * n:GA0 + 12 + 2 * n, :], ps[4 + n % 4][:, :], ACT.Sqrt,
                               bias=eps[:, :]).then_inc(norm_root, 1)
            act.wait_ge(v_t, 1)
            act.activation(vt[:, :, :], ps[6][:, :], ACT.Copy).then_inc(v_out, 1)
            act.activation(z[:, CB0:CB0 + CT_T, :], z[:, CB0:CB0 + CT_T, :], ACT.Sigmoid).then_inc(cb_sig, 1)
            act.wait_ge(v_out, 1)
            act.wait_ge(q_ready, 5)
            with act.Fori(0, N_GATE // 2) as m:
                for h in range(2):
                    u = U_GATE + h * U_D
                    for k in range(U_D):
                        ahead(u, k, m, 2 * U_D)
                        if k == 0:
                            act.activation(taps_now[:, :], conv_wT[:, m * 2 + h, :], ACT.Copy).then_inc(now_ready, 1)
                            act.activation(q_now[:, :], z[:, m * 2 + h, :], ACT.Copy).then_inc(now_ready, 1)
                            act.activation(sink_now[:, :], sinks[:, bass.ds(m * 4 + 2 * h, 2)], ACT.Copy
                                           ).then_inc(now_ready, 1)
                            act.activation(bias_now[:, :, :], bias[:, bass.ds(m * 4 + 2 * h, 2), :], ACT.Copy
                                           ).then_inc(now_ready, 1)
                            act.activation(v_now[:, :, HEAD:2 * HEAD], vt[:, :, bass.ds(m * HEAD, HEAD)],
                                           ACT.Copy).then_inc(now_ready, 1)
                        if k == 3:
                            act.wait_ge(neg_ready, m * 2 + (h + 1))
                            for hd in range(2):
                                for b, cols in enumerate((slice(0, P), slice(P, 3 * P))):
                                    n = 2 * hd + b
                                    act.activation(logit[:, hd, cols], logit[:, hd, cols], ACT.Exp,
                                                   bias=s_neg[:, n:n + 1], accum_out=s_den[:, n:n + 1])
                            act.activation(s_sink, s_sink, ACT.Exp).then_inc(exp_ready, 1)
                        if k == 5:
                            act.wait_ge(pt_done, m * 2 + (h + 1))
                            for hd in range(2):
                                act.activation(probT[:, hd, :], ps[6 + hd][:, :3 * P], ACT.Copy
                                               ).then_inc(pt_out, 1)
                    hold(act, o_done, m * 2 + (h + 1), cleared)
                    act.activation(attn[:, m * 2 + h, :], ps[4][:, :TOK], ACT.Copy).then_inc(o_hi, 1)
                    lows(m * (2 * GT) + (T_GATE + h * GT), m * 6 + (T_GATE // GT + h) * 3,
                         m * (2 * U_D) + (u + U_D + RING))

            act.wait_ge(centered, 1)
            act.activation(conv_sq[:, :, :], z[:, CA0:CA0 + CT_T, :], ACT.Square).then_inc(csq_ready, 1)
            act.wait_ge(var_sum, 1)
            act.activation(rstd[:, :], ps[5][:, :TOK], ACT.Sqrt, bias=eps[:, :], scale=1.0 / CONV_C
                           ).then_inc(croot, 1)
            act.wait_ge(cnorm, 1)
            for t in range(CT_T):
                act.activation(z[:, CA0 + t, :], z[:, CA0 + t, :], ACT.Silu, bias=lb_col[:, t:t + 1],
                               scale=lg_col[:, t:t + 1]).then_inc(silu_ready, 1)
            for t in range(CT_T):
                act.wait_ge(silu_ready, t + 1)
                act.activation(conv[:, t, 0, :], z[:, CA0 + t, :], ACT.Copy).then_inc(chi, 1)
            act.wait_ge(bank_free, T_MERGE + 4)
            with act.Fori(0, 4) as g:
                for n in range(2):
                    u = U_MERGE + n * U_H
                    for k in range(U_H):
                        ahead(u, k, g, 2 * U_H)
                        if n == 0 and k < 2:
                            gate = z[:, bass.ds(g * GT + (GA0, GC0)[k], GT), :]
                            act.activation(gate, gate, ACT.Sigmoid).then_inc(gate_sig, 1)
                    lows(g * (2 * GT) + (T_MERGE + n * GT), g * 6 + (T_MERGE // GT + n) * 3,
                         g * (2 * U_H) + (u + U_H + RING))
                for t in range(GT):
                    hold(act, m_val, g * GT + (t + 1), cleared)
                    act.activation(hs[:, g * GT + t, 0, :], val[t][:, :], ACT.Copy).then_inc(m_hi, 1)
            with act.Fori(0, 4) as g:
                for k in range(U_D):
                    ahead(U_MIX, k, g, U_D)
                lows(g * GT + T_MIX, g * 3 + T_MIX // GT * 3, g * U_D + (U_MIX + U_D + RING))
                for t in range(GT):
                    hold(act, x2_ready, g * GT + (t + 1), cleared)
                    act.activation(val[t][:, :], xT[:, g * GT + t, :], ACT.Square).then_inc(x2_sq, 1)
            act.wait_ge(sum_ready, 2)
            act.activation(rstd[:, :], ps[4][:, :TOK], ACT.Sqrt, bias=eps[:, :], scale=1.0 / D
                           ).then_inc(root_ready, 1)
            for t in range(KT):
                high_h(KT, t, 3 * KT)
            with act.Fori(0, 11) as g:
                for n in range(2):
                    u = U_FIN + n * U_D
                    for k in range(U_D):
                        ahead(u, k, g, 2 * U_D)
                    lows(g * (2 * GT) + (T_FIN + n * GT), g * 6 + (T_FIN // GT + n) * 3,
                         g * (2 * U_D) + (u + U_D + RING))
                    for t in range(GT):
                        if n == 0:
                            act.wait_ge(bank_free, g * (2 * GT) + (T_FIN + GT + t + 1))
                            act.activation(val[t][:, :], val[t][:, :], ACT.Silu).then_inc(g_silu, 1)
                        else:
                            hold(act, f_val, g * GT + (t + 1), cleared)
                            act.activation(hid[:, g * GT + t, 0, :], up[t][:, :], ACT.Copy).then_inc(f_hi, 1)
            def rows(g):
                act.wait_ge(o_t, g + 1)
                for b in range(2):
                    act.activation(out_rows[g][:, b, :], ps[4 + b][:, :], ACT.Copy).then_inc(rows_ready, 1)

            for g in range(4):
                for k in range(U_F):
                    ahead(U_FOUT + g * U_F, k)
                    if g and k == 7:
                        rows(g - 1)
                lows(T_FOUT + g * GT, (T_FOUT // GT + g) * 3, U_FOUT + (g + 1) * U_F + RING)
            rows(3)

        @block.vector
        def _(dve):
            me = Steps(dve, dve_self)

            def split_low(number, slot):
                dve.wait_ge(hi_ready, number + 1)
                dve.tensor_tensor(w_lo[slot][:, :, :], raw[slot][:, :, :], w_hi[slot][:, :, :].bitcast(f32),
                                  ALU.subtract).then_inc(w_split, 1)

            def ahead(first, k, i=0, per=0):
                n = first + k + LEAD
                if n < U_END:
                    split_low(i * per + n, n % RING)

            def leave(tile, to):
                for t in range(GT):
                    dve.wait_ge(low_ready, tile + (t + 1))
                    dve.tensor_tensor(to(t), ps[t][:, :TOK], low[t % 2][:, :], ALU.add).then_inc(bank_free, 1)

            def ada_unit(first, k, i=0, per=U_D, slots=ada, acc=acc, done=acc_done):
                n = first + k
                dve.wait_ge(ada_here[n % RING], i * (per // RING * 16) + (n // RING + 1) * 16)
                for a in range(UK):
                    kt = UK * k + a
                    rows = slots[n % RING][:, a, :]
                    to = done if kt == KT - 1 else acc
                    if kt == 0:
                        ins = dve.tensor_scalar(acc[:, :], rows, c_col[:, 0:1], None, ALU.mult)
                    else:
                        if a == 0:
                            dve.wait_ge(ada_free, i * per + (n + RING))
                        else:
                            me.wait()
                        ins = dve.scalar_tensor_tensor(out=to[:, :], in0=rows, scalar=c_col[:, kt:kt + 1],
                                                       in1=acc[:, :], op0=ALU.mult, op1=ALU.add)
                    if a == 0:
                        me.step(ins)
                    else:
                        ins.then_inc(ada_free, 1)

            def mod_out(count, col, tiles=GT):
                dve.wait_ge(mod_sum, count)
                me.step(dve.tensor_tensor(mod[:, bass.ds(col, tiles)], ps[7][:, 0:tiles],
                                          rowsT[:, bass.ds(col + 16, tiles)], ALU.add))

            for n, s in enumerate((w_split, w_used, ada_free, bank_free)):
                dve.memset(gain[:, n:n + 1], 0.0).then_inc(s, RING)
            dve.wait_ge(rows_t, 1)
            dve.tensor_copy(conv_wT[:, :, 0:CONV_W],
                            ps[5][:, 0:CT_T * 32].rearrange("p (t j) -> p t j", j=32)[:, :, 0:CONV_W])
            dve.tensor_copy(rowsT[:, :], ps[4][:, 0:168]).then_inc(rows_out, 1)
            dve.wait_ge(rows_out, 1)
            me.step(dve.tensor_copy(conv_wT[:, :, CONV_W:CONV_W + 1],
                                    cb_col.rearrange("p (t o) -> p t o", o=1)))
            dve.wait_ge(cleared, CLEARS)
            dve.tensor_copy(table[:, P:2 * P], ps[6][0:HEADS, :P]).then_inc(table_ready, 1)
            dve.wait_ge(small_here, SMALL * 16)
            me.step(dve.tensor_scalar(qk_g[:, 0:1], qk_g[:, 0:1], HEAD ** -0.5, None, ALU.mult))
            dve.wait_ge(c_ready, 1)

            def h_value(first, t):
                dve.scalar_tensor_tensor(out=xn[:, t, :], in0=xT[:, t, :], scalar=gain[:, t:t + 1],
                                         in1=rstd[:, :], op0=ALU.mult, op1=ALU.mult).then_inc(h_val, 1)

            def h_split(first, t, shift):
                dve.wait_ge(h_val, first + t + 1)
                dve.wait_ge(h_hi, first + t + 1)
                dve.scalar_tensor_tensor(out=hs[:, t, 1, :], in0=xn[:, t, :],
                                         scalar=mod[:, shift + t:shift + t + 1],
                                         in1=hs[:, t, 0, :].bitcast(f32), op0=ALU.add, op1=ALU.subtract
                                         ).then_inc(h_ready, 1)

            for half in range(2):
                for g in me.each(2, U_D + 1):
                    for k in range(U_D):
                        ada_unit(half * LEAD_U // 2, k, g, U_D, wide_ada, wide_acc, wide_done)
                    mod_out(g + (half * 2 + 1), g * KT + half * KT // 2, 2 * GT)
                if half == 0:
                    dve.wait_ge(root_ready, 1)
                    me.step(dve.reciprocal(rstd[:, :], rstd[:, :]))
                else:
                    ahead(U_PROJ - LEAD, 0)
                tiles = range(half * KT // 2, (half + 1) * KT // 2)
                now = slice(tiles[0], tiles[-1] + 1)
                me.wait()
                me.step(dve.scalar_tensor_tensor(out=gain[:, now], in0=mod[:, KT + now.start:KT + now.stop],
                                                 scalar=1.0, in1=g_mix[:, now], op0=ALU.add, op1=ALU.mult))
                me.wait()
                for t in tiles:
                    h_value(0, t)
                    if t >= tiles[2]:
                        h_split(0, t - 2, 0)
                    if t in (10, 12):
                        ahead(U_PROJ - LEAD, 1 + (10, 12).index(t))
                for t in tiles[-2:]:
                    h_split(0, t, 0)
            for g in me.each(N_PROJ, U_D + 1):
                for k in range(U_D):
                    if k == 3:
                        mod_out(g + (LEAD_ADA // 2 + 1), g * GT + (LEAD_ADA - 1) * GT)
                    ahead(U_PROJ, k, g, U_D)
                    ada_unit(A_PROJ, k, g)
                leave(g * GT + T_PROJ, lambda t: z[:, g * GT + t, :])
            mod_out(LEAD_ADA // 2 + N_PROJ + 1, (LEAD_ADA + N_PROJ - 1) * GT)

            for n in range(5):
                part, root = z[:, 2 * n:2 * n + 2, :], z[:, GA0 + 10 + 2 * n:GA0 + 12 + 2 * n, :]
                dve.wait_ge(norm_root, n + 1)
                me.step(dve.reciprocal(root, root))
                me.wait()
                dve.scalar_tensor_tensor(out=part, in0=part, scalar=qk_g[:, n // 4:n // 4 + 1], in1=root,
                                         op0=ALU.mult, op1=ALU.mult).then_inc(q_ready, 1)
            dve.wait_ge(swapped, 1)
            dve.wait_ge(q_ready, 5)
            sw = ps[5][:, :].rearrange("p (t n) -> p t n", n=TOK)
            dve.tensor_copy(kz[0:HEAD, 0, 0:KV:2, :], z[0:HEAD, K0:V0, :])
            dve.tensor_copy(kz[0:HEAD, 0, 1:KV:2, :], sw[0:HEAD, :, :])
            dve.tensor_copy(kz[HEAD:P, 1, 1:KV:2, :], z[HEAD:P, K0:V0, :])
            dve.tensor_copy(kz[HEAD:P, 1, 0:KV:2, :], sw[HEAD:P, :, :]).then_inc(k_padded, 1)
            dve.wait_ge(cb_sig, 1)

            per = 2 * (1 + (CONV_W - 1) + 3 + 2)
            for m in me.each(N_GATE // 2, per):
                for h in range(2):
                    n = m * 2 + h
                    u = U_GATE + h * U_D
                    tap = 0
                    for k in range(U_D):
                        ahead(u, k, m, 2 * U_D)
                        if k == 0:
                            me.step(dve.tensor_tensor(padded[:, CONV_W - 1:], z[:, m * 2 + (CA0 + h), :],
                                                      z[:, m * 2 + (CB0 + h), :], ALU.mult))
                            dve.wait_ge(now_ready, m * 10 + (5 * h + 5))
                        if k == 2:
                            dve.wait_ge(s_done, m * 2 + (h + 1))
                            me.step(dve.memset(s_rec, 0.0))
                            for hd in range(2):
                                for b, (cols, keys) in enumerate(((slice(0, P), slice(P, 2 * P)),
                                                                  (slice(P, 3 * P), slice(0, 2 * P)))):
                                    ins = dve.tensor_tensor_reduce(
                                        out=logit[:, hd, cols], in0=ps[4 + hd][:, cols], in1=bias_now[:, hd, keys],
                                        scale=1.0, scalar=sink_now[:, hd:hd + 1], op0=ALU.add, op1=ALU.max,
                                        accum_out=s_max[:, 2 * hd + b:2 * hd + b + 1])
                            me.step(ins)
                            me.wait()
                            me.step(dve.tensor_scalar(s_neg, s_max, -1.0, None, ALU.mult))
                            me.wait()
                            dve.tensor_tensor(s_sink.rearrange("p (h b) -> p h b", b=2),
                                              s_neg.rearrange("p (h b) -> p h b", b=2),
                                              sink_now[:, :, None].broadcast_to([P, 2, 2]), ALU.add
                                              ).then_inc(neg_ready, 1)
                        if k == 4:
                            dve.wait_ge(exp_ready, m * 2 + (h + 1))
                            me.step(dve.tensor_tensor(s_den, s_den, s_sink, ALU.add))
                            me.wait()
                            me.step(dve.reciprocal(s_rec, s_den))
                            me.wait()
                            for hd in range(2):
                                for b, cols in enumerate((slice(0, P), slice(P, 3 * P))):
                                    ins = dve.tensor_scalar(logit[:, hd, cols], logit[:, hd, cols],
                                                            s_rec[:, 2 * hd + b:2 * hd + b + 1], None, ALU.mult)
                            ins.then_inc(p_ready, 1)
                        for tap in range(sum(TAPS[:k]), sum(TAPS[:k + 1])):
                            me.wait()
                            now = padded[:, tap:tap + TOK]
                            if tap == 0:
                                me.step(dve.tensor_scalar(conv_acc[:, :], now, taps_now[:, 0:1],
                                                          taps_now[:, CONV_W:CONV_W + 1], ALU.mult, ALU.add))
                            elif tap < CONV_W - 1:
                                me.step(dve.scalar_tensor_tensor(
                                    out=conv_acc[:, :], in0=now, scalar=taps_now[:, tap:tap + 1],
                                    in1=conv_acc[:, :], op0=ALU.mult, op1=ALU.add))
                            else:
                                dve.scalar_tensor_tensor(
                                    out=z[:, m * 2 + (CA0 + h), :], in0=now, scalar=taps_now[:, tap:tap + 1],
                                    in1=conv_acc[:, :], op0=ALU.mult, op1=ALU.add).then_inc(conv_out, 1)
                    dve.wait_ge(o_hi, m * 2 + (h + 1))
                    dve.tensor_tensor(attn[:, m * 2 + (CB0 + h), :], ps[4][:, :TOK],
                                      attn[:, m * 2 + h, :].bitcast(f32), ALU.subtract).then_inc(o_out, 1)
                    leave(m * (2 * GT) + (T_GATE + h * GT),
                          lambda t: z[:, m * (2 * GT) + (GA0 + h * GT + t), :])

            wide = z[:, CA0:CA0 + CT_T, :]
            dve.wait_ge(mean_sum, 1)
            me.step(dve.tensor_scalar(usum[:, :], ps[4][:, :TOK], 1.0 / CONV_C, None, ALU.mult))
            me.wait()
            dve.tensor_tensor(wide, wide, usum[:, None, :].broadcast_to([P, CT_T, TOK]), ALU.subtract
                              ).then_inc(centered, 1)
            me.step(dve.memset(acc_done, 0.0))
            dve.wait_ge(croot, 1)
            me.step(dve.reciprocal(rstd[:, :], rstd[:, :]))
            me.wait()
            dve.tensor_tensor(wide, wide, rstd[:, None, :].broadcast_to([P, CT_T, TOK]), ALU.mult
                              ).then_inc(cnorm, 1)
            for t in range(CT_T):
                dve.wait_ge(chi, t + 1)
                dve.tensor_tensor(conv[:, t, 1, :], z[:, CA0 + t, :], conv[:, t, 0, :].bitcast(f32),
                                  ALU.subtract).then_inc(conv_ready, 1)
            for g in me.each(4, 2 * GT):
                for n in range(2):
                    u, tile = U_MERGE + n * U_H, g * (2 * GT) + (T_MERGE + n * GT)
                    for k in range(U_H):
                        ahead(u, k, g, 2 * U_H)
                        if n == 0:
                            a = A_MERGE + k
                            dve.wait_ge(ada_here[k], g * 16 + (a // RING + 1) * 16)
                            dve.wait_ge(ada_free, g * 4 + (a + RING))
                            dve.scalar_tensor_tensor(
                                out=acc_done, in0=ada[k][:, 0, :], scalar=c_col[:, bass.ds(g * 4 + k, 1)],
                                in1=acc_done, op0=ALU.mult, op1=ALU.add).then_inc(ada_free, 1)
                    leave(tile, lambda t: val[t][:, :])
                    dve.wait_ge(gate_sig, g * 2 + (n + 1))
                    for t in range(GT):
                        ga, gc = z[:, g * GT + (GA0 + t), :], z[:, g * GT + (GC0 + t), :]
                        dve.wait_ge(bank_free, tile + (t + 1 + GT))
                        if n == 0:
                            me.step(dve.tensor_tensor(ga, val[t][:, :], ga, ALU.mult))
                        else:
                            me.step(dve.tensor_tensor(val[t][:, :], val[t][:, :], gc, ALU.mult))
                            me.wait()
                            dve.tensor_tensor(val[t][:, :], val[t][:, :], ga, ALU.add).then_inc(m_val, 1)
                for t in range(GT):
                    dve.wait_ge(m_hi, g * GT + (t + 1))
                    dve.tensor_tensor(hs[:, g * GT + t, 1, :], val[t][:, :], hs[:, g * GT + t, 0, :].bitcast(f32),
                                      ALU.subtract).then_inc(m_ready, 1)
            me.step(dve.memset(usum[:, :], 0.0))
            for g in me.each(4, U_D + GT - 1 + 1):
                for k in range(U_D):
                    if k == 3:
                        mod_out(g + 13, g * GT + 15 * GT)
                    ahead(U_MIX, k, g, U_D)
                    ada_unit(A_MIX, k, g)
                tile = g * GT + T_MIX
                leave(tile, lambda t: val[t][:, :])
                for t in range(GT):
                    xt = xT[:, g * GT + t, :]
                    dve.wait_ge(bank_free, tile + (t + 1 + GT))
                    dve.scalar_tensor_tensor(out=xt, in0=val[t][:, :], scalar=mod[:, bass.ds(g * GT + (2 * KT + t), 1)],
                                             in1=xt, op0=ALU.mult, op1=ALU.add).then_inc(x2_ready, 1)
                for t in range(GT):
                    dve.wait_ge(x2_sq, g * GT + (t + 1))
                    me.wait()
                    ins = dve.tensor_tensor(usum[:, :], usum[:, :], val[t][:, :], ALU.add)
                    if t < GT - 1:
                        me.step(ins)
                    else:
                        ins.then_inc(sq_summed, 1)
                        dve.wait_ge(sq_summed, g + 1)
            mod_out(17, 19 * GT)
            me.wait()
            me.step(dve.scalar_tensor_tensor(out=gain[:, :], in0=mod[:, 4 * KT:5 * KT], scalar=1.0, in1=g_ffn,
                                             op0=ALU.add, op1=ALU.mult))
            dve.wait_ge(root_ready, 2)
            me.step(dve.reciprocal(rstd[:, :], rstd[:, :]))
            me.wait()
            for t in range(KT):
                h_value(KT, t)
                if t >= 2:
                    h_split(KT, t - 2, 3 * KT)
            for t in (KT - 2, KT - 1):
                h_split(KT, t, 3 * KT)
            with dve.Fori(0, 11) as g:
                for n in range(2):
                    u, tile = U_FIN + n * U_D, g * (2 * GT) + (T_FIN + n * GT)
                    for k in range(U_D):
                        ahead(u, k, g, 2 * U_D)
                    leave(tile, lambda t: (val, up)[n][t][:, :])
                for t in range(GT):
                    dve.wait_ge(g_silu, g * GT + (t + 1))
                    dve.wait_ge(bank_free, tile + (t + 1 + GT))
                    dve.tensor_tensor(up[t][:, :], up[t][:, :], val[t][:, :], ALU.mult).then_inc(f_val, 1)
                for t in range(GT):
                    dve.wait_ge(f_hi, g * GT + (t + 1))
                    dve.tensor_tensor(hid[:, g * GT + t, 1, :], up[t][:, :], hid[:, g * GT + t, 0, :].bitcast(f32),
                                      ALU.subtract).then_inc(f_ready, 1)
            for g in range(4):
                for k in range(U_F):
                    ahead(U_FOUT + g * U_F, k)
                    if k < U_D:
                        ada_unit(A_FOUT + g * U_D, k, done=acc)
                    if k == 12:
                        mod_out(18 + g, (20 + g) * GT)
                tile = T_FOUT + g * GT
                leave(tile, lambda t: val[t][:, :])
                if g:
                    dve.wait_ge(o_t, g)
                me.wait()
                for t in range(GT):
                    col = 5 * KT + g * GT + t
                    dve.wait_ge(bank_free, tile + t + 1 + GT)
                    dve.scalar_tensor_tensor(out=out_t[:, t, :], in0=val[t][:, :], scalar=mod[:, col:col + 1],
                                             in1=xT[:, g * GT + t, :], op0=ALU.mult, op1=ALU.add
                                             ).then_inc(o_val, 1)

        @block.tensor
        def _(pe):
            def unit(first, k, of, tile, moving, i=0, per=0, ready=None):
                n = first + k
                if ready:
                    pe.wait_ge(ready[0], ready[1] + UK * (k + 1))
                pe.wait_ge(w_split, i * per + (n + 1 + RING))
                for t in range(GT):
                    if k == 0:
                        pe.wait_ge(bank_free, tile + (t + 1))
                    for a in range(UK):
                        w = slice(t * P, (t + 1) * P)
                        both = moving(UK * k + a)
                        pe.matmul(ps[t][:, :], w_hi[n % RING][:, a, w], both, start=(k == 0 and a == 0), stop=False)
                        mm = pe.matmul(ps[t][:, :TOK], w_lo[n % RING][:, a, w], both[:, 0, :], start=False,
                                       stop=(k == of - 1 and a == UK - 1))
                    if k == of - 1 and t < GT - 1:
                        mm.then_inc(tile_done, 1)
                mm.then_inc(w_used, 1)

            def ada_sum(used, what, tiles=GT):
                pe.wait_ge(ada_free, used)
                for t in range(tiles):
                    mm = pe.matmul(ps[7][:, t:t + 1], what[:, t * P:(t + 1) * P], ones[:, 0:1], start=True, stop=True)
                mm.then_inc(mod_sum, 1)

            def h_tile(kt):
                return hs[:, kt, :, :]

            def attn_tile(kt):
                return attn[:, kt:kt + CB0 + 1:CB0, :]

            def conv_tile(kt):
                return conv[:, kt, :, :]

            def hid_tile(kt):
                return hid[:, kt, :, :]

            pe.wait_ge(small_here, SMALL * 16)
            pe.transpose(ps[4][:, 0:112], rows1[:, :], ident[0:112, 0:112])
            pe.transpose(ps[4][:, 112:168], rows2[:, :], ident[0:56, 0:56])
            for t in range(CT_T):
                pe.transpose(ps[5][:, t * 32:t * 32 + CONV_W], taps_rows[:, t * P:(t + 1) * P],
                             ident[0:CONV_W, 0:CONV_W])
            pe.matmul(ps[6][0:HEADS, :P], rel[:, :], buckets[:, :], start=True, stop=True).then_inc(rows_t, 1)
            pe.wait_ge(x_here, 32)
            for b in range(KT // 2):
                if b >= 4:
                    pe.wait_ge(xsq_ready, b - 3)
                for t in range(2):
                    for r in range(2):
                        col = t * TOK + r * P
                        tr = pe.transpose(ps[b % 4][:, col:col + P], xtok[:, r, (2 * b + t) * P:(2 * b + t + 1) * P],
                                          ident)
                tr.then_inc(xt_done, 1)
            pe.wait_ge(cleared, CLEARS)
            pe.wait_ge(rows_out, 1)
            for t in range(KT):
                if t % 2 == 0:
                    pe.wait_ge(xsq_ready, t // 2 + 1)
                mm = pe.matmul(ps[4][:, :TOK], ones[:, :], xsq[:, t, :], start=(t == 0), stop=(t == KT - 1))
            mm.then_inc(sum_ready, 1)
            with pe.Fori(0, 2) as g:
                ada_sum(g * U_D + (U_D + RING), wide_done, 2 * GT)
            pe.wait_ge(bias_here, 16)
            for b in range(HEADS // 2):
                if b >= 2:
                    pe.wait_ge(bias_out, b - 1)
                pe.matmul(ps[5 + b % 2][:, :], flip, reversed_bias[:, 2 * b:2 * b + 2, :], start=True, stop=True
                          ).then_inc(flipped, 1)
            with pe.Fori(0, 2) as g:
                ada_sum(g * U_D + (3 * U_D + RING), wide_done, 2 * GT)
            with pe.Fori(0, N_PROJ) as g:
                for k in range(U_D):
                    if k == 2:
                        ada_sum(g * U_D + (A_PROJ + RING), acc_done)
                    unit(U_PROJ, k, U_D, g * GT + T_PROJ, h_tile, g, U_D, (h_ready, 0))
            ada_sum(A_MERGE + RING, acc_done)

            for n in range(5):
                pe.wait_ge(norm_sq, n + 1)
                if n == 4:
                    pe.wait_ge(norm_root, 1)
                if n == 3:
                    pe.wait_ge(mod_sum, LEAD_ADA // 2 + N_PROJ + 1)
                    pe.wait_ge(q_ready, 1)
                pe.matmul(ps[4 + n % 4][:, :], head_mean, z[:, GA0 + 2 * n:GA0 + 2 * n + 2, :], start=True,
                          stop=True).then_inc(norm_ms, 1)
            pe.wait_ge(norm_root, 3)
            for b in range(2):
                for t in range(2):
                    tr = pe.transpose(ps[6][:, (2 * b + t) * P:(2 * b + t + 1) * P], z[:, V0 + t, b * P:(b + 1) * P],
                                      ident)
            tr.then_inc(v_t, 1)
            pe.wait_ge(q_ready, 5)
            pe.matmul(ps[5][:, :], swap, z[:, K0:V0, :], start=True, stop=True).then_inc(swapped, 1)
            pe.wait_ge(k_padded, 1)
            with pe.Fori(0, N_GATE // 2) as m:
                for h in range(2):
                    n = m * 2 + (h + 1)
                    u, tile = U_GATE + h * U_D, m * (2 * GT) + (T_GATE + h * GT)
                    for k in range(U_D):
                        if k == 1:
                            pe.wait_ge(now_ready, m * 10 + (5 * h + 5))
                            for hd in range(2):
                                pe.matmul(ps[4 + hd][:, 0:P], q_now[:, 0:P], kz[:, hd, m, 0:P], start=True, stop=True)
                                mm = pe.matmul(ps[4 + hd][:, P:3 * P], q_now[:, P:2 * P], kz[:, hd, m, :], start=True,
                                               stop=True)
                            mm.then_inc(s_done, 1)
                        if k == 5:
                            pe.wait_ge(p_ready, n)
                            for hd in range(2):
                                for c in range(3):
                                    tr = pe.transpose(ps[6 + hd][:, c * P:(c + 1) * P], logit[:, hd, c * P:(c + 1) * P],
                                                      ident)
                            tr.then_inc(pt_done, 1)
                        if k == 7:
                            pe.wait_ge(pt_out, n * 2)
                            for b, parts in enumerate((((0, 0),), ((1, 0), (2, 1)))):
                                last = (1, parts[-1])
                                for hd in range(2):
                                    for c, keys in parts:
                                        v = v_now[:, keys, HEAD:3 * HEAD] if hd == 0 else v_now[:, keys, 0:2 * HEAD]
                                        mm = pe.matmul(ps[4][:, b * P:(b + 1) * P], v, probT[:, hd, c * P:(c + 1) * P],
                                                       start=(hd == 0 and (c, keys) == parts[0]),
                                                       stop=((hd, (c, keys)) == last))
                            mm.then_inc(o_done, 1)
                        unit(u, k, U_D, tile, h_tile, m, 2 * U_D)

            pe.wait_ge(conv_out, CT_T)
            pe.wait_ge(o_out, HEADS // 2)
            for t in range(CT_T):
                mm = pe.matmul(ps[4][:, :TOK], ones[:, :], z[:, CA0 + t, :], start=(t == 0), stop=(t == CT_T - 1))
            mm.then_inc(mean_sum, 1)
            pe.wait_ge(csq_ready, 1)
            for t in range(CT_T):
                mm = pe.matmul(ps[5][:, :TOK], ones[:, :], conv_sq[:, t, :], start=(t == 0), stop=(t == CT_T - 1))
            mm.then_inc(var_sum, 1)
            with pe.Fori(0, 4) as g:
                for k in range(U_H):
                    unit(U_MERGE, k, U_H, g * (2 * GT) + T_MERGE, attn_tile, g, 2 * U_H)
                for k in range(U_H):
                    unit(U_MERGE + U_H, k, U_H, g * (2 * GT) + (T_MERGE + GT), conv_tile, g, 2 * U_H, (conv_ready, 0))
            with pe.Fori(0, 4) as g:
                for k in range(U_D):
                    if k == 2:
                        ada_sum(g * U_D + (A_MIX + RING), acc_done)
                    unit(U_MIX, k, U_D, g * GT + T_MIX, h_tile, g, U_D, (m_ready, 0))
            ada_sum(A_MIX + 4 * U_D + RING, acc_done)
            pe.wait_ge(sq_summed, 4)
            pe.matmul(ps[4][:, :TOK], ones[:, :], usum[:, :], start=True, stop=True).then_inc(sum_ready, 1)
            with pe.Fori(0, 11) as g:
                for n in range(2):
                    for k in range(U_D):
                        unit(U_FIN + n * U_D, k, U_D, g * (2 * GT) + (T_FIN + n * GT), h_tile, g, 2 * U_D,
                             (h_ready, KT) if n == 0 else None)

            def to_rows(n):
                pe.wait_ge(o_val, n)
                for b in range(2):
                    for t in range(GT):
                        tr = pe.transpose(ps[4 + b][:, t * P:(t + 1) * P], out_t[:, t, b * P:(b + 1) * P], ident)
                tr.then_inc(o_t, 1)

            with pe.Fori(0, 2) as m:
                for h in range(2):
                    for k in range(U_F):
                        if k == 11:
                            ada_sum(m * (2 * U_D) + (A_FOUT + (h + 1) * U_D + RING), acc)
                        if k == 5 and h == 1:
                            to_rows(m * (2 * GT) + GT)
                        unit(U_FOUT + h * U_F, k, U_F, m * (2 * GT) + (T_FOUT + h * GT), hid_tile, m, 2 * U_F,
                             (f_ready, 0) if h == 0 else None)
                to_rows(m * (2 * GT) + 2 * GT)


def kernel(x, c, w_ada, b_ada, norm_mix_g, w_in, q_norm_g, k_norm_g, attn_sinks, rel_bias, w_attn_out,
           conv_w, conv_b, conv_ln_g, conv_ln_b, w_conv_out, w_mix_out, norm_ffn_g, w_ffn_in, w_ffn_out):
    import math

    import numpy as np
    import concourse.bacc as bacc
    from concourse.bass_utils import run_bass_kernel_spmd

    p = np.arange(P)
    squares = np.zeros((P, 4, P), np.float32)
    squares[p, 0, p] = 1
    squares[p, 1, P - 1 - p] = 1
    squares[p, 2, (p + HEAD) % P] = 1
    squares[:, 3, :] = (p[:, None] // HEAD == p[None, :] // HEAD) / HEAD
    onehot = np.zeros((32, P), np.float32)
    for j in range(P):
        dist = P - 1 - j
        bucket = dist if dist < 16 else min(31, 16 + int(math.log(dist / 16) / math.log(P / 16) * 16))
        onehot[bucket, j] = 1

    arrays = {
        "x": x[0], "c": c.reshape(16, P), "w_ada": w_ada[0], "b_ada": b_ada.reshape(96, P),
        "norm_mix_g": norm_mix_g.reshape(16, P), "w_in": w_in[0], "q_norm_g": q_norm_g.reshape(HEAD, 1),
        "k_norm_g": k_norm_g.reshape(HEAD, 1), "attn_sinks": attn_sinks.reshape(1, HEADS),
        "rel_bias": rel_bias, "w_attn_out": w_attn_out[0], "conv_w": conv_w[0],
        "conv_b": conv_b.reshape(8, P), "conv_ln_g": conv_ln_g.reshape(8, P),
        "conv_ln_b": conv_ln_b.reshape(8, P), "w_conv_out": w_conv_out[0], "w_mix_out": w_mix_out[0],
        "norm_ffn_g": norm_ffn_g.reshape(16, P), "w_ffn_in": w_ffn_in[0], "w_ffn_out": w_ffn_out[0],
        "squares": squares, "onehot": onehot,
    }
    arrays = {name: np.ascontiguousarray(a) for name, a in arrays.items()}
    nc = bacc.Bacc("TRN2", target_bir_lowering=False, num_devices=1, dynamic_dma_scratch_size=1024)
    args = {name: nc.dram_tensor(f"in_{name}", a.shape, mybir.dt.from_np(a.dtype), kind="ExternalInput").ap()
            for name, a in arrays.items()}
    out = nc.dram_tensor("out", (TOK, D), f32, kind="ExternalOutput").ap()
    build(nc, *args.values(), out)
    result = run_bass_kernel_spmd(nc, [{f"in_{name}": a for name, a in arrays.items()}], core_ids=[0])
    return result.results[0]["out"].reshape(1, TOK, D)
```

```python
from contextlib import ExitStack

import concourse.bass as bass
from concourse import mybir

f32 = mybir.dt.float32
f32r = mybir.dt.float32r
ALU = mybir.AluOpType
ACT = mybir.ActivationFunctionType

P = 128
D = 2048
TOK = 256
HEAD = 64
HEADS = 16
KV = 4
CONV_W = 31
CONV_C = D // 2
DFF = 5632
EPS = 1e-6
MASKED = -1.0e30
COLS = 512
GT = COLS // P
UK = 2
KT = D // P
AT_T = HEADS * HEAD // P
CT_T = CONV_C // P
FT = DFF // P
RING = 4
LEAD = 3
U_D = KT // UK
U_H = AT_T // UK
U_F = FT // UK
Q0, K0, V0, CA0, CB0, GA0, GC0 = 0, 8, 10, 12, 20, 28, 44
Z_T = 60
N_PROJ = 7
N_GATE = 8
LEAD_ADA = 8
WIDE = 2 * COLS
U_PROJ = 0
U_GATE = U_PROJ + N_PROJ * U_D
U_MERGE = U_GATE + N_GATE * U_D
U_CONV = U_MERGE + 4 * U_H
U_MIX = U_CONV + 4 * U_H
U_FIN = U_MIX + 4 * U_D
U_FOUT = U_FIN + 11 * 2 * U_D
U_END = U_FOUT + 4 * U_F
T_PROJ = 0
T_GATE = T_PROJ + N_PROJ * GT
T_MERGE = T_GATE + N_GATE * GT
T_CONV = T_MERGE + 4 * GT
T_MIX = T_CONV + 4 * GT
T_FIN = T_MIX + 4 * GT
T_FOUT = T_FIN + 11 * 2 * GT
LEAD_U = LEAD_ADA // 2 * U_D
A_PROJ = LEAD_U
A_MERGE = A_PROJ + N_PROJ * U_D
A_CONV = A_MERGE + U_D
A_MIX = A_CONV + KT
A_FOUT = A_MIX + 3 * U_D
SMALL = 9
CLEARS = 6
TAPS = [4, 5, 4, 5, 5, 4, 4, 0]


class Steps:

    def __init__(self, eng, sem):
        self.eng, self.sem, self.n, self.round = eng, sem, 0, 0

    def step(self, ins):
        ins.then_inc(self.sem, 1)
        self.n += 1

    def wait(self, upto=None):
        self.eng.wait_ge(self.sem, self.round + (self.n if upto is None else upto))

    def each(self, rounds, per):
        at = self.n
        with self.eng.Fori(0, rounds) as i:
            self.round = i * per
            yield i
            assert self.n - at == per, f"{self.n - at} steps a round, not {per}"
        self.round = 0
        self.n = at + rounds * per


def hold(eng, sem, value, started):
    eng.wait_ge(started, 1)
    eng.wait_ge(sem, value)


def build(nc, x, w_ada, w_in, vectors, taps, q_norm_g, k_norm_g, attn_sinks, rel_bias, w_attn_out,
          w_conv_out, w_mix_out, w_ffn_in, w_ffn_out, squares, onehot, out):
    toeplitz = nc.dram_tensor("toeplitz_rows", (HEADS, 3 * P), f32, kind="Internal")

    with ExitStack() as ctx:
        base = 1152
        at = {"free": base}

        def place(name, shape, dt=f32, offset=None):
            size = 4
            for s in shape[1:]:
                size *= s
            if offset is None:
                offset = at["free"]
                at["free"] += (size + 31) // 32 * 32
            return nc.alloc_sbuf_tensor_at(name, shape, dt, offset=offset)

        def sem(name):
            return ctx.enter_context(nc.semaphore(name))

        raw = [place(f"raw{s}", [P, UK, COLS]) for s in range(RING)]
        w_hi = [place(f"w_hi{s}", [P, UK, COLS], f32r) for s in range(RING)]
        lead_off = at["free"]
        w_lo = [place(f"w_lo{s}", [P, UK, COLS], f32r) for s in range(RING)]
        ada = [place(f"ada{s}", [P, UK, COLS]) for s in range(RING)]
        wide_ada = [place(f"wide_ada{s}", [P, UK, WIDE], offset=lead_off + s * UK * WIDE * 4) for s in range(RING)]
        hs_off = at["free"]
        hs = place("h_split", [P, KT, 2, TOK], f32r)
        xT = place("xT", [P, KT, TOK])
        sq4 = place("squares", [P, 4, P])
        ident, flip, swap, head_mean = (sq4[:, n, :] for n in range(4))
        ones = place("ones", [P, P])
        rowsT = place("vectors", [P, 160])
        conv_wT = place("conv_wT", [P, CT_T, 32])
        mod = place("mod", [P, 96])
        gain = place("gain", [P, KT])
        ao = at["free"]
        acc = place("ada_acc", [P, COLS])
        low = [place(f"low{s}", [P, TOK]) for s in range(2)]
        vo = at["free"]
        val = [place(f"val{s}", [P, TOK]) for s in range(GT)]
        probT = place("probT", [P, 2, 3 * P], offset=vo)
        usum = place("sum_sq", [P, TOK])
        rstd = place("rstd", [P, TOK])
        qk_g = place("qk_gain", [P, 5])
        sinks = place("sinks", [P, HEADS])
        padded = place("conv_padded", [P, CONV_W - 1 + TOK])
        conv_acc = place("conv_acc", [P, 2, TOK], offset=ao)
        taps_now = place("taps_now", [P, 32])
        v_now = place("v_now", [P, 2, 3 * HEAD])
        sink_now = place("sink_now", [P, 2])
        stats = place("softmax_stats", [P, 5, 4])
        s_max, s_neg, s_den, s_sink, s_rec = (stats[:, n, :] for n in range(5))
        uo = at["free"]
        q_now = place("q_now", [P, TOK])
        logit = place("logit", [P, 2, 3 * P])
        up = [place(f"up{s}", [P, TOK], offset=uo + s * TOK * 4) for s in range(GT)]
        wide_done = place("wide_acc_done", [P, WIDE], offset=uo)
        acc_done = wide_done[:, COLS:]
        eps = place("eps", [P, 1])
        zo = at["free"]
        z = place("z", [P, Z_T, TOK], offset=zo)
        attn = place("attn_split", [P, CB0 + CT_T, TOK], f32r, offset=zo)
        norm_in = z[:, GA0:GA0 + 2, :]
        rms_rows = z[:, GA0 + 2:GA0 + 4, :].rearrange("p t n -> p (t n)")
        token_rms = stats[:, 1, 0:2]
        rms = stats[:, 0:2, :]
        xn = place("xn", [P, KT, TOK], offset=zo + GA0 * TOK * 4)
        xtok = place("x_rows", [P, 2, D], offset=zo)
        bo = zo + Z_T * TOK * 4
        bias = place("bias", [P, HEADS, 2 * P], offset=bo)
        conv_sq = place("conv_sq", [P, CT_T, TOK], offset=bo)
        conv = place("conv_split", [P, CT_T, 2, TOK], f32r, offset=bo)
        ko = bo + 4 * HEADS * 2 * P
        kz = place("k_padded", [P, 2, KV, TOK], offset=ko)
        vt = place("v_rows", [P, 2, KV * HEAD], offset=ko + 8192)
        bias_now = place("bias_now", [P, 2, 2 * P], offset=ko + 10240)
        wide_acc = place("wide_acc", [P, WIDE], offset=zo + 50 * TOK * 4)
        hid = place("hidden_split", [P, FT, 2, TOK], f32r, offset=zo)
        end = zo + 4 * FT * 2 * TOK
        assert ko + 12288 <= end
        assert end <= 229344, end
        out_t = place("out_t", [P, GT, TOK], offset=hs_off)
        out_rows = [place(f"out_rows{s}", [P, 2, COLS], offset=hs_off + 4096 * (1 + s)) for s in range(4)]
        reversed_bias = place("reversed_bias", [P, HEADS, 2 * P], offset=hs_off)
        table = place("bias_table", [HEADS, 3 * P], offset=hs_off + 16384)
        rel = place("rel", [32, HEADS], offset=hs_off + 24576)
        buckets = place("buckets", [32, P], offset=hs_off + 25600)
        xsq = place("x_sq", [P, KT, TOK], offset=bo)

        ps = [ctx.enter_context(nc.psum_tensor(f"ps{b}", [P, 512], f32)) for b in range(8)]

        c_col = rowsT[:, 0:16]
        b_ada_col = rowsT[:, 16:112]
        g_mix, g_ffn = rowsT[:, 112:128], rowsT[:, 128:144]
        lg_col, lb_col = rowsT[:, 144:152], rowsT[:, 152:160]

        raw_here = [sem(f"raw_here{s}") for s in range(RING)]
        hi_ready = sem("hi_ready")
        w_split = sem("w_split")
        w_used = sem("w_used")
        ada_here = [sem(f"ada_here{s}") for s in range(RING)]
        ada_free = sem("ada_free")
        tile_done = sem("tile_done")
        low_ready = sem("low_ready")
        bank_free = sem("bank_free")
        act_self, dve_self, pool_self = sem("act_self"), sem("dve_self"), sem("pool_self")
        small_here, x_here, const_here = sem("small_here"), sem("x_here"), sem("const_here")
        rows_t = sem("bias_of_distance")
        table_sum, table_ready, table_stored, bias_here = (
            sem("table_sum"), sem("table_ready"), sem("table_stored"), sem("bias_here"))
        flipped, bias_out = sem("flipped"), sem("bias_out")
        xt_done, xt_out = sem("xt_done"), sem("xt_out")
        cleared = sem("cleared")
        xsq_ready, sum_ready, ms_ready, root_ready = (
            sem("xsq_ready"), sem("sum_ready"), sem("ms_ready"), sem("root_ready"))
        mod_sum, c_here, c_ready = sem("mod_sum"), sem("vectors_here"), sem("c_ready")
        h_val, h_hi, h_ready = sem("h_val"), sem("h_hi"), sem("h_ready")
        z_out = sem("z_out")
        norm_sq, norm_ms, norm_root, k_ready = (
            sem("norm_sq"), sem("norm_ms"), sem("norm_root"), sem("k_ready"))
        swapped, k_padded, v_t, v_out, cb_sig = (
            sem("swapped"), sem("k_padded"), sem("v_t"), sem("v_out"), sem("cb_sig"))
        q_ready, norm_rec, norm_wide = sem("q_ready"), sem("norm_rec"), sem("norm_wide")
        norm_rows = sem("norm_rows")
        now_ready, s_done, neg_ready, exp_ready, rec_ready, p_ready = (
            sem("now_ready"), sem("s_done"), sem("neg_ready"), sem("exp_ready"), sem("rec_ready"),
            sem("p_ready"))
        pt_done, pt_out, o_done, o_hi, o_out = (
            sem("pt_done"), sem("pt_out"), sem("o_done"), sem("o_hi"), sem("o_out"))
        conv_out, mean_sum, centered, csq_ready, var_sum, croot, cnorm, silu_ready, chi, conv_ready = (
            sem("conv_out"), sem("mean_sum"), sem("centered"), sem("csq_ready"), sem("var_sum"),
            sem("croot"), sem("cnorm"), sem("silu_ready"), sem("conv_hi"), sem("conv_ready"))
        gated_ready = sem("gated_ready")
        gate_sig, m_val, m_hi, m_ready = sem("gate_sig"), sem("m_val"), sem("m_hi"), sem("m_ready")
        x2_ready, x2_sq = sem("x2_ready"), sem("x2_sq")
        sq_summed, zero_ready, token_ready, rms_wide = (
            sem("sq_summed"), sem("zero_ready"), sem("token_ready"), sem("rms_wide"))
        g_silu, f_val, f_hi, f_ready = sem("g_silu"), sem("f_val"), sem("f_hi"), sem("f_ready")
        o_val, o_t, rows_ready, stored = sem("o_val"), sem("o_t"), sem("rows_ready"), sem("stored")

        block = ctx.enter_context(nc.Block())

        @block.sync
        def _(sp):
            def weights(u, w, row, col):
                number, slot = u
                sp.wait_ge(w_split, number + 1)
                sp.dma_start(raw[slot][:, :, :],
                             w[row:row + UK * P, bass.ds(col, COLS)].rearrange("(a p) n -> p a n", p=P)
                             ).then_inc(raw_here[slot], 16)

            def ada_unit(number, slot, row, col):
                sp.wait_ge(ada_free, number + 1)
                sp.dma_start(ada[slot][:, :, :],
                             w_ada[bass.ds(row, UK * P), bass.ds(col, COLS)].rearrange("(a p) n -> p a n", p=P)
                             ).then_inc(ada_here[slot], 16)

            sp.dma_start(rowsT[:, :], vectors).then_inc(c_here, 16)
            for half in range(2):
                with sp.Fori(0, 2) as n:
                    for k in range(U_D):
                        sp.wait_ge(ada_free, n * U_D + (half * LEAD_U // 2 + k + 1))
                        sp.dma_start(wide_ada[k % RING][:, :, :],
                                     w_ada[k * UK * P:(k + 1) * UK * P, bass.ds(n * D + half * WIDE, WIDE)]
                                     .rearrange("(a p) n -> p a n", p=P)).then_inc(ada_here[k % RING], 16)
            for k in range(LEAD):
                weights((U_PROJ + k, k), w_in, k * UK * P, 0)
            with sp.Fori(0, N_PROJ) as g:
                for k in range(U_D):
                    n = k + LEAD
                    weights((g * U_D + (U_PROJ + n), n % RING), w_in, n % U_D * UK * P, (g + n // U_D) * COLS)
                    if k == 0:
                        sp.wait_ge(ada_free, LEAD_U + RING)
                    ada_unit(g * U_D + (A_PROJ + k), k % RING, k * UK * P, g * COLS + LEAD_ADA * COLS)
            for k in range(LEAD, U_D):
                weights((U_GATE + k, k % RING), w_in, k * UK * P, N_PROJ * COLS)
            with sp.Fori(1, N_GATE) as g:
                for k in range(U_D):
                    weights((g * U_D + (U_GATE + k), k % RING), w_in, k * UK * P, g * COLS + N_PROJ * COLS)
            for k in range(4 * U_H):
                weights((U_MERGE + k, k % RING), w_attn_out, k % U_H * UK * P, k // U_H * COLS)
                a = k - LEAD - 1
                if 0 <= a < U_D:
                    ada_unit(A_MERGE + a, a % RING, a * UK * P, 15 * COLS)
            def late_ada(g, k):
                sp.wait_ge(ada_free, g * 4 + (A_CONV + k + 1))
                sp.dma_start(ada[k][:, 0, :], w_ada[bass.ds((g * 4 + k) * P, P), 16 * COLS:17 * COLS]
                             ).then_inc(ada_here[k], 16)

            for k in range(LEAD):
                weights((U_CONV + k, k), w_conv_out, k * UK * P, 0)
            with sp.Fori(0, 3) as g:
                for k in range(U_H):
                    n = k + LEAD
                    weights((g * U_H + (U_CONV + n), n % RING), w_conv_out, n % U_H * UK * P, (g + n // U_H) * COLS)
                    late_ada(g, k)
            weights((U_CONV + 3 * U_H + LEAD, LEAD), w_conv_out, LEAD * UK * P, 3 * COLS)
            late_ada(3, 0)
            for k in range(LEAD):
                weights((U_MIX + k, k), w_mix_out, k * UK * P, 0)
                late_ada(3, k + 1)

            with sp.Fori(0, 3) as g:
                for k in range(U_D):
                    n = k + LEAD
                    weights((g * U_D + (U_MIX + n), n % RING), w_mix_out, n % U_D * UK * P, (g + n // U_D) * COLS)
                    ada_unit(g * U_D + (A_MIX + k), k % RING, k * UK * P, (g + 17) * COLS)
            for k in range(LEAD, U_D):
                weights((U_MIX + 3 * U_D + k, k % RING), w_mix_out, k * UK * P, 3 * COLS)
            with sp.Fori(0, 11) as g:
                for n in range(2):
                    for k in range(U_D):
                        weights((g * (2 * U_D) + (U_FIN + n * U_D + k), k % RING), w_ffn_in,
                                k * UK * P, g * COLS + n * DFF)
            with sp.Fori(0, 2) as g:
                for h in range(2):
                    for k in range(U_F):
                        weights((g * (2 * U_F) + (U_FOUT + h * U_F + k), (h * U_F + k) % RING), w_ffn_out,
                                k * UK * P, g * (2 * COLS) + h * COLS)
                        a = k - LEAD
                        if 0 <= a < U_D:
                            ada_unit(g * (2 * U_D) + (A_FOUT + h * U_D + a), a % RING, a * UK * P,
                                     g * (2 * COLS) + (20 + h) * COLS)
            for g in range(4):
                sp.wait_ge(rows_ready, 2 * (g + 1))
                sp.dma_start(out[:, g * COLS:(g + 1) * COLS].rearrange("(b p) n -> p b n", p=P),
                             out_rows[g][:, :, :]).then_inc(stored, 16)
            sp.wait_ge(stored, 4 * 16)

        @block.gpsimd
        def _(pool):
            pool.memset(ones[:, :], 1.0).then_inc(cleared, 1)
            pool.memset(eps[:, :], EPS).then_inc(cleared, 1)
            pool.memset(table[:, :], MASKED).then_inc(cleared, 1)
            pool.memset(padded[:, :], 0.0).then_inc(cleared, 1)
            pool.memset(v_now[:, :, :], 0.0).then_inc(cleared, 1)
            pool.memset(kz[:, :, :, :], 0.0).then_inc(cleared, 1)

        @block.scalar
        def _(act):
            def split_high(number, slot, turn):
                act.wait_ge(raw_here[slot], turn)
                act.wait_ge(w_used, number + 1)
                act.activation(w_hi[slot][:, :, :], raw[slot][:, :, :], ACT.Copy).then_inc(hi_ready, 1)

            def ahead(first, k, i=0, per=0):
                n = first + k + LEAD
                if n < U_END:
                    split_high(i * per + n, n % RING, i * (per // RING * 16) + (n // RING + 1) * 16)

            def lows(tile, groups3, used):
                for t in range(GT):
                    if t < GT - 1:
                        act.wait_ge(tile_done, groups3 + (t + 1))
                    else:
                        act.wait_ge(w_used, used)
                    act.wait_ge(bank_free, tile + (t + 3))
                    act.activation(low[t % 2][:, :], ps[t][:, TOK:], ACT.Copy).then_inc(low_ready, 1)

            def out_of_banks(tile, groups3, used, to):
                for t in range(GT):
                    if t < GT - 1:
                        hold(act, tile_done, groups3 + (t + 1), cleared)
                    else:
                        hold(act, w_used, used, cleared)
                    act.activation(to(t), ps[t][:, :TOK], ACT.Copy).then_inc(bank_free, 1)

            act.dma_start(sq4[:, :, :], squares).then_inc(small_here, 16)
            act.dma_start(rel[:, :], rel_bias).then_inc(small_here, 16)
            act.dma_start(buckets[:, :], onehot).then_inc(small_here, 16)
            act.wait_ge(c_here, 16)
            act.activation(c_col, c_col, ACT.Silu).then_inc(c_ready, 1)
            act.dma_start(conv_wT[:, :, :], taps).then_inc(small_here, 16)
            for n, v in ((0, q_norm_g), (4, k_norm_g)):
                for h in range(2):
                    act.dma_start(qk_g[h * HEAD:(h + 1) * HEAD, n:n + 1], v).then_inc(small_here, 16)
            act.dma_start(sinks[:, :], attn_sinks.broadcast_to([P, HEADS])).then_inc(small_here, 16)
            for b in range(2):
                act.dma_start(xtok[:, b, :], x[b * P:(b + 1) * P, :]).then_inc(x_here, 16)
            act.wait_ge(rows_t, 1)
            act.wait_ge(cleared, CLEARS)
            act.activation(table[:, P:2 * P], ps[6][0:HEADS, :P], ACT.Copy).then_inc(table_ready, 1)
            act.wait_ge(table_ready, 1)
            act.dma_start(toeplitz.ap(), table[:, :]).then_inc(table_stored, 16)
            act.wait_ge(table_stored, 16)
            shifted = bass.AP(toeplitz.ap().tensor, 0, [[1, P], [3 * P, HEADS], [1, 2 * P]])
            act.dma_start(reversed_bias[:, :, :], shifted).then_inc(bias_here, 16)
            for b in range(KT // 2):
                act.wait_ge(xt_done, b + 1)
                act.activation(xT[:, 2 * b:2 * b + 2, :], ps[b % 4][:, :], ACT.Copy)
                act.activation(xsq[:, 2 * b:2 * b + 2, :], ps[b % 4][:, :], ACT.Square).then_inc(xsq_ready, 1)
            act.wait_ge(sum_ready, 1)
            act.wait_ge(cleared, CLEARS)
            act.activation(rstd[:, :], ps[4][:, :TOK], ACT.Sqrt, bias=eps[:, :], scale=1.0 / D
                           ).then_inc(root_ready, 1)
            for b in range(HEADS // 2):
                act.wait_ge(flipped, b + 1)
                act.activation(bias[:, 2 * b:2 * b + 2, :], ps[5 + b % 2][:, :], ACT.Copy).then_inc(bias_out, 1)

            def high_h(first, t, shift):
                act.wait_ge(h_val, first + t + 1)
                act.activation(hs[:, t, 0, :], xn[:, t, :], ACT.Identity, bias=mod[:, shift + t:shift + t + 1]
                               ).then_inc(h_hi, 1)

            for t in range(KT // 2):
                high_h(0, t, 0)
            for n in range(LEAD):
                ahead(U_PROJ - LEAD, n)
            for t in range(KT // 2, KT):
                high_h(0, t, 0)
            with act.Fori(0, 2) as g:
                for k in range(U_D - 1):
                    ahead(U_PROJ, k, g, U_D)
                out_of_banks(g * GT + T_PROJ, g * 3 + T_PROJ // GT * 3, g * U_D + (U_PROJ + U_D + RING),
                             lambda t: z[:, g * GT + t, :])
                ahead(U_PROJ, U_D - 1, g, U_D)
            with act.Fori(0, N_PROJ - 2) as g:
                for k in range(U_D - 1):
                    ahead(U_PROJ + 2 * U_D, k, g, U_D)
                    if k == 0:
                        act.activation(norm_in, z[:, bass.ds(g * 2, 2), :], ACT.Square).then_inc(norm_sq, 1)
                    if k == 3:
                        hold(act, norm_ms, g + 1, cleared)
                        act.activation(rms, ps[4][:, 0:8].rearrange("p (n h) -> p n h", h=4), ACT.Sqrt,
                                       bias=eps[:, :]).then_inc(norm_root, 1)
                    if k == 5:
                        hold(act, norm_rec, g + 1, cleared)
                        act.activation(rms_rows.rearrange("p (n e) -> p n e", e=HEAD),
                                       rms.rearrange("p t n -> p (t n)")[:, :, None].broadcast_to([P, 8, HEAD]),
                                       ACT.Copy).then_inc(norm_rows, 1)
                out_of_banks(g * GT + (T_PROJ + 2 * GT), g * 3 + 6, g * U_D + (U_PROJ + 3 * U_D + RING),
                             lambda t: z[:, g * GT + (2 * GT + t), :])
                ahead(U_PROJ + 2 * U_D, U_D - 1, g, U_D)

            act.wait_ge(v_t, 1)
            act.activation(vt[:, :, :], ps[6][:, :], ACT.Copy).then_inc(v_out, 1)
            act.wait_ge(bank_free, T_GATE + GT)
            act.activation(z[:, CB0:CB0 + CT_T, :], z[:, CB0:CB0 + CT_T, :], ACT.Sigmoid).then_inc(cb_sig, 1)
            act.activation(s_rec, sinks[:, 0:4], ACT.Exp, scale=0.0).then_inc(cb_sig, 1)
            act.wait_ge(v_out, 1)
            act.wait_ge(q_ready, 1)
            with act.Fori(0, N_GATE // 2) as m:
                for h in range(2):
                    u = U_GATE + h * U_D
                    for k in range(U_D - 1):
                        if k not in (0, 3, 5, 6):
                            ahead(u, k, m, 2 * U_D)
                        if k == 0:
                            act.activation(q_now[:, :], z[:, m * 2 + h, :], ACT.Copy).then_inc(now_ready, 1)
                            act.activation(sink_now[:, :], sinks[:, bass.ds(m * 4 + 2 * h, 2)], ACT.Copy
                                           ).then_inc(now_ready, 1)
                            act.activation(bias_now[:, :, :], bias[:, bass.ds(m * 4 + 2 * h, 2), :], ACT.Copy
                                           ).then_inc(now_ready, 1)
                            act.activation(v_now[:, :, HEAD:2 * HEAD], vt[:, :, bass.ds(m * HEAD, HEAD)],
                                           ACT.Copy).then_inc(now_ready, 1)
                            hold(act, conv_out, m * 2 + (h + 1), cleared)
                            act.activation(taps_now[:, :], conv_wT[:, m * 2 + h, :], ACT.Copy).then_inc(now_ready, 1)
                        if k == 3:
                            act.wait_ge(neg_ready, m * 2 + (h + 1))
                            for hd in range(2):
                                for b, cols in enumerate((slice(0, P), slice(P, 3 * P))):
                                    n = 2 * hd + b
                                    act.activation(logit[:, hd, cols], logit[:, hd, cols], ACT.Exp,
                                                   bias=s_neg[:, n:n + 1], accum_out=s_den[:, n:n + 1])
                            act.activation(s_sink, s_sink, ACT.Exp).then_inc(exp_ready, 1)
                        if k == 5:
                            hold(act, rec_ready, m * 2 + (h + 1), cleared)
                            for hd in range(2):
                                for b, cols in enumerate((slice(0, P), slice(P, 3 * P))):
                                    n = 2 * hd + b
                                    ins = act.activation(logit[:, hd, cols], logit[:, hd, cols], ACT.Copy,
                                                         scale=s_rec[:, n:n + 1])
                            ins.then_inc(p_ready, 1)
                        if k == 6:
                            act.wait_ge(pt_done, m * 2 + (h + 1))
                            for hd in range(2):
                                act.activation(probT[:, hd, :], ps[6 + hd][:, :3 * P], ACT.Copy
                                               ).then_inc(pt_out, 1)
                        if k in (0, 3, 5, 6):
                            ahead(u, k, m, 2 * U_D)
                    hold(act, o_done, m * 2 + (h + 1), cleared)
                    act.activation(attn[:, m * 2 + h, :], ps[4][:, :TOK], ACT.Copy).then_inc(o_hi, 1)
                    out_of_banks(m * (2 * GT) + (T_GATE + h * GT), m * 6 + (T_GATE // GT + h) * 3,
                                 m * (2 * U_D) + (u + U_D + RING),
                                 lambda t: z[:, m * (2 * GT) + (GA0 + h * GT + t), :])
                    ahead(u, U_D - 1, m, 2 * U_D)

            for k in range(4 * U_H):
                if k % U_H == U_H - 1:
                    g = k // U_H
                    if g:
                        act.wait_ge(gated_ready, g * GT)
                    out_of_banks(T_MERGE + g * GT, (T_MERGE // GT + g) * 3, U_MERGE + (g + 1) * U_H + RING,
                                 lambda t: val[t][:, :])
                ahead(U_MERGE, k)
                if k == 0:
                    act.wait_ge(bank_free, T_MERGE + GT)
                if k in (0, 1, 3, 4):
                    gate = z[:, GA0 + (0, 1, 0, 2, 3)[k] * GT:GA0 + (1, 2, 0, 3, 4)[k] * GT, :]
                    act.activation(gate, gate, ACT.Sigmoid).then_inc(gate_sig, 1)
                if k == 3:
                    act.wait_ge(centered, 1)
                    act.activation(conv_sq[:, :, :], z[:, CA0:CA0 + CT_T, :], ACT.Square).then_inc(csq_ready, 1)
                if k == 6:
                    act.wait_ge(var_sum, 1)
                    act.activation(rstd[:, :], ps[5][:, :TOK], ACT.Sqrt, bias=eps[:, :], scale=1.0 / CONV_C
                                   ).then_inc(croot, 1)
                if k in (8, 9):
                    act.wait_ge(cnorm, 1)
                    for t in range((k - 8) * 4, (k - 7) * 4):
                        act.activation(z[:, CA0 + t, :], z[:, CA0 + t, :], ACT.Silu, bias=lb_col[:, t:t + 1],
                                       scale=lg_col[:, t:t + 1]).then_inc(silu_ready, 1)
                if k in (10, 11):
                    for t in range((k - 10) * 4, (k - 9) * 4):
                        act.wait_ge(silu_ready, t + 1)
                        act.activation(conv[:, t, 0, :], z[:, CA0 + t, :], ACT.Copy).then_inc(chi, 1)
                if k >= 12:
                    gate = z[:, GC0 + (k - 12) * GT:GC0 + (k - 11) * GT, :]
                    act.activation(gate, gate, ACT.Sigmoid).then_inc(gate_sig, 1)
            def merged_high(i, at):
                for t in range(GT):
                    hold(act, m_val, i * GT + (at * GT + t + 1), cleared)
                    act.activation(hs[:, i * GT + (at * GT + t), 0, :], val[t][:, :], ACT.Copy).then_inc(m_hi, 1)

            def squares_of(i, at):
                for t in range(GT):
                    hold(act, x2_ready, i * GT + (at * GT + t + 1), cleared)
                    act.activation(val[t][:, :], xT[:, i * GT + (at * GT + t), :], ACT.Square).then_inc(x2_sq, 1)

            def group(u, tile, units, i, at, free, after=None, last=None):
                for k in range(units - 1):
                    ahead(u + at * units, k, i, units)
                    if k == 0 and after:
                        after(i, at - 1)
                if free:
                    hold(act, *free(i), cleared)
                out_of_banks(i * GT + (tile + at * GT), i * 3 + (tile // GT + at) * 3,
                             i * units + (u + (at + 1) * units + RING), lambda t: val[t][:, :])
                if last:
                    last()
                ahead(u + at * units, units - 1, i, units)

            group(U_CONV, T_CONV, U_H, 0, 0, lambda i: (gated_ready, 4 * GT))
            with act.Fori(0, 3) as i:
                group(U_CONV, T_CONV, U_H, i, 1, lambda i: (m_ready, (i + 1) * GT), merged_high)
            group(U_MIX, T_MIX, U_D, 0, 0, lambda i: (m_ready, 4 * GT), lambda i, at: merged_high(0, 3))
            with act.Fori(0, 2) as i:
                group(U_MIX, T_MIX, U_D, i, 1, lambda i: (sq_summed, i + 1), squares_of)
            act.activation(s_rec, eps[:, 0:1].broadcast_to([P, 4]), ACT.Sqrt).then_inc(act_self, 1)
            group(U_MIX, T_MIX, U_D, 0, 3, lambda i: (sq_summed, 3), squares_of, lambda: squares_of(0, 3))
            act.wait_ge(sq_summed, 4)
            act.activation(token_rms, ps[4][:, 0:2], ACT.Sqrt, bias=eps[:, :], scale=1.0 / D
                           ).then_inc(root_ready, 1)
            for t in range(2 * UK):
                high_h(KT, t, 3 * KT)

            def gate_and_up(g, at, with_h=False):
                for n in range(2):
                    u = U_FIN + (2 * at + n) * U_D
                    for k in range(U_D):
                        if with_h and n == 0 and UK * k + 2 * UK < KT:
                            high_h(KT, UK * k + 2 * UK, 3 * KT)
                            high_h(KT, UK * k + 2 * UK + 1, 3 * KT)
                        ahead(u, k, g, 2 * U_D)
                    lows(g * (2 * GT) + (T_FIN + (2 * at + n) * GT), g * 6 + (T_FIN // GT + 2 * at + n) * 3,
                         g * (2 * U_D) + (u + U_D + RING))
                    for t in range(GT):
                        if n == 0:
                            act.wait_ge(bank_free, g * (2 * GT) + (T_FIN + (2 * at + 1) * GT + t + 1))
                            act.activation(val[t][:, :], val[t][:, :], ACT.Silu).then_inc(g_silu, 1)
                        else:
                            hold(act, f_val, g * GT + (at * GT + t + 1), cleared)
                            act.activation(hid[:, g * GT + (at * GT + t), 0, :], up[t][:, :], ACT.Copy
                                           ).then_inc(f_hi, 1)

            gate_and_up(0, 0, True)
            with act.Fori(0, 10) as g:
                gate_and_up(g, 1)

            def rows(g):
                act.wait_ge(o_t, g + 1)
                for b in range(2):
                    act.activation(out_rows[g][:, b, :], ps[4 + b][:, :], ACT.Copy).then_inc(rows_ready, 1)

            for g in range(4):
                for k in range(U_F):
                    ahead(U_FOUT + g * U_F, k)
                    if g and k == 7:
                        rows(g - 1)
                lows(T_FOUT + g * GT, (T_FOUT // GT + g) * 3, U_FOUT + (g + 1) * U_F + RING)
            rows(3)

        @block.vector
        def _(dve):
            me = Steps(dve, dve_self)

            def split_low(number, slot):
                dve.wait_ge(hi_ready, number + 1)
                dve.tensor_tensor(w_lo[slot][:, :, :], raw[slot][:, :, :], w_hi[slot][:, :, :].bitcast(f32),
                                  ALU.subtract).then_inc(w_split, 1)

            def ahead(first, k, i=0, per=0):
                n = first + k + LEAD
                if n < U_END:
                    split_low(i * per + n, n % RING)

            def leave(tile, to):
                for t in range(GT):
                    dve.wait_ge(low_ready, tile + (t + 1 - T_FIN))
                    dve.tensor_tensor(to(t), ps[t][:, :TOK], low[t % 2][:, :], ALU.add).then_inc(bank_free, 1)

            def ada_unit(first, k, i=0, per=U_D, slots=ada, acc=acc, done=acc_done):
                n = first + k
                dve.wait_ge(ada_here[n % RING], i * (per // RING * 16) + (n // RING + 1) * 16)
                for a in range(UK):
                    kt = UK * k + a
                    rows = slots[n % RING][:, a, :]
                    to = done if kt == KT - 1 else acc
                    if kt == 0:
                        dve.wait_ge(ada_free, i * per + (n + RING))
                        ins = dve.tensor_scalar(acc[:, :], rows, c_col[:, 0:1], None, ALU.mult)
                    else:
                        if a == 0:
                            dve.wait_ge(ada_free, i * per + (n + RING))
                        else:
                            me.wait()
                        ins = dve.scalar_tensor_tensor(out=to[:, :], in0=rows, scalar=c_col[:, kt:kt + 1],
                                                       in1=acc[:, :], op0=ALU.mult, op1=ALU.add)
                    if a == 0:
                        me.step(ins)
                    else:
                        ins.then_inc(ada_free, 1)

            def mod_out(count, col, tiles=GT):
                dve.wait_ge(mod_sum, count)
                me.step(dve.tensor_tensor(mod[:, bass.ds(col, tiles)], ps[7][:, 0:tiles],
                                          rowsT[:, bass.ds(col + 16, tiles)], ALU.add))

            for n, s in enumerate((w_split, w_used, ada_free, bank_free)):
                dve.memset(gain[:, n:n + 1], 0.0).then_inc(s, RING)
            dve.memset(gain[:, 4:5], 0.0).then_inc(o_out, 1)
            dve.memset(gain[:, 5:6], 0.0).then_inc(conv_out, 1)
            dve.wait_ge(c_ready, 1)

            def h_value(first, t, rms=rstd):
                dve.scalar_tensor_tensor(out=xn[:, t, :], in0=xT[:, t, :], scalar=gain[:, t:t + 1],
                                         in1=rms[:, :], op0=ALU.mult, op1=ALU.mult).then_inc(h_val, 1)

            def h_split(first, t, shift):
                dve.wait_ge(h_val, first + t + 1)
                dve.wait_ge(h_hi, first + t + 1)
                dve.scalar_tensor_tensor(out=hs[:, t, 1, :], in0=xn[:, t, :],
                                         scalar=mod[:, shift + t:shift + t + 1],
                                         in1=hs[:, t, 0, :].bitcast(f32), op0=ALU.add, op1=ALU.subtract
                                         ).then_inc(h_ready, 1)

            def gains(half):
                now = slice(half * KT // 2, (half + 1) * KT // 2)
                me.wait()
                me.step(dve.scalar_tensor_tensor(out=gain[:, now], in0=mod[:, KT + now.start:KT + now.stop],
                                                 scalar=1.0, in1=g_mix[:, now], op0=ALU.add, op1=ALU.mult))
                me.wait()

            for g in range(4):
                for k in range(U_D):
                    ada_unit(g * U_D, k, 0, U_D, wide_ada, wide_acc, wide_done)
                    if g and k == 2:
                        half, n = divmod(g - 1, 2)
                        mod_out(g, n * KT + half * KT // 2, 2 * GT)
                    if g == 1 and k == 5:
                        dve.wait_ge(root_ready, 1)
                        me.step(dve.reciprocal(rstd[:, :], rstd[:, :]))
                    if g == 2 and k == 2:
                        gains(0)
                    if g == 2 and k >= 3 or g == 3 and k < 3:
                        t = k - 3 + (g - 2) * U_D
                        h_value(0, t)
                        if t >= 2:
                            h_split(0, t - 2, 0)
            ahead(U_PROJ - LEAD, 0)
            h_split(0, KT // 2 - 2, 0)
            h_split(0, KT // 2 - 1, 0)
            ahead(U_PROJ - LEAD, 1)
            dve.wait_ge(small_here, SMALL * 16)
            me.step(dve.tensor_scalar(qk_g[:, 0:1], qk_g[:, 0:1], HEAD ** -0.5, None, ALU.mult))
            me.wait()
            me.step(dve.tensor_copy(qk_g[:, 1:4], qk_g[:, 0:1].broadcast_to([P, 3])))
            mod_out(4, KT + KT // 2, 2 * GT)
            gains(1)
            for t in range(KT // 2, KT):
                h_value(0, t)
                if t >= KT // 2 + 2:
                    h_split(0, t - 2, 0)
                if t == 11:
                    ahead(U_PROJ - LEAD, 2)
            h_split(0, KT - 2, 0)
            h_split(0, KT - 1, 0)
            def proj(g, first, norms):
                for k in range(U_D):
                    if k == 6:
                        mod_out(g + (first + LEAD_ADA // 2 + 1), g * GT + (first + LEAD_ADA - 1) * GT)
                    ahead(U_PROJ + first * U_D, k, g, U_D)
                    ada_unit(A_PROJ + first * U_D, k, g)
                    if norms and k == 4:
                        dve.wait_ge(norm_root, g + 1)
                        dve.reciprocal(rms, rms).then_inc(norm_rec, 1)
                    if norms and k == 6:
                        part = z[:, bass.ds(g * 2, 2), :]
                        dve.wait_ge(norm_wide, g + 1)
                        me.step(dve.scalar_tensor_tensor(
                            out=part, in0=part, scalar=qk_g[:, bass.ds(g, 1)],
                            in1=ps[4][:, :].rearrange("p (t n) -> p t n", n=TOK), op0=ALU.mult, op1=ALU.mult))

            for g in me.each(2, U_D + 1):
                proj(g, 0, False)
            for g in me.each(N_PROJ - 2, U_D + 2):
                proj(g, 2, True)

            me.wait()
            dve.memset(gain[:, 0:1], 0.0).then_inc(q_ready, 1)
            dve.wait_ge(swapped, 1)
            sw = ps[5][:, :].rearrange("p (t n) -> p t n", n=TOK)
            dve.tensor_copy(kz[0:HEAD, 0, 0:KV:2, :], z[0:HEAD, K0:V0, :])
            dve.tensor_copy(kz[0:HEAD, 0, 1:KV:2, :], sw[0:HEAD, :, :])
            dve.tensor_copy(kz[HEAD:P, 1, 1:KV:2, :], z[HEAD:P, K0:V0, :])
            dve.tensor_copy(kz[HEAD:P, 1, 0:KV:2, :], sw[HEAD:P, :, :]).then_inc(k_padded, 1)
            mod_out(LEAD_ADA // 2 + N_PROJ + 1, (LEAD_ADA + N_PROJ - 1) * GT)
            dve.wait_ge(cb_sig, 2)

            per = 2 * (1 + CONV_W + 3 + 1)
            for m in me.each(N_GATE // 2, per):
                for h in range(2):
                    n = m * 2 + h
                    u = U_GATE + h * U_D
                    tap = 0
                    for k in range(U_D):
                        if k == U_D - 1:
                            me.wait()
                            dve.tensor_tensor(z[:, m * 2 + (CA0 + h), :], conv_acc[:, 0, :], conv_acc[:, 1, :],
                                              ALU.add).then_inc(conv_out, 1)
                        if k != 2:
                            ahead(u, k, m, 2 * U_D)
                        if k == U_D - 1:
                            dve.wait_ge(o_hi, m * 2 + (h + 1))
                            dve.tensor_tensor(attn[:, m * 2 + (CB0 + h), :], ps[4][:, :TOK],
                                              attn[:, m * 2 + h, :].bitcast(f32), ALU.subtract).then_inc(o_out, 1)
                        if k == 0:
                            me.step(dve.tensor_tensor(padded[:, CONV_W - 1:], z[:, m * 2 + (CA0 + h), :],
                                                      z[:, m * 2 + (CB0 + h), :], ALU.mult))
                            dve.wait_ge(now_ready, m * 10 + (5 * h + 5))
                        if k == 2:
                            dve.wait_ge(s_done, m * 2 + (h + 1))
                            me.step(dve.memset(s_rec, 0.0))
                            for hd in range(2):
                                for b, (cols, keys) in enumerate(((slice(0, P), slice(P, 2 * P)),
                                                                  (slice(P, 3 * P), slice(0, 2 * P)))):
                                    ins = dve.tensor_tensor_reduce(
                                        out=logit[:, hd, cols], in0=ps[4 + hd][:, cols], in1=bias_now[:, hd, keys],
                                        scale=1.0, scalar=sink_now[:, hd:hd + 1], op0=ALU.add, op1=ALU.max,
                                        accum_out=s_max[:, 2 * hd + b:2 * hd + b + 1])
                            me.step(ins)
                            me.wait()
                            me.step(dve.tensor_scalar(s_neg, s_max, -1.0, None, ALU.mult))
                            me.wait()
                            dve.tensor_tensor(s_sink.rearrange("p (h b) -> p h b", b=2),
                                              s_neg.rearrange("p (h b) -> p h b", b=2),
                                              sink_now[:, :, None].broadcast_to([P, 2, 2]), ALU.add
                                              ).then_inc(neg_ready, 1)
                        if k == 2:
                            ahead(u, k, m, 2 * U_D)
                        if k == 3:
                            dve.wait_ge(exp_ready, m * 2 + (h + 1))
                            me.step(dve.tensor_tensor(s_den, s_den, s_sink, ALU.add))
                            me.wait()
                            dve.reciprocal(s_rec, s_den).then_inc(rec_ready, 1)
                        if k == 0:
                            glu = me.n
                            last = [glu, glu]
                        for tap in range(sum(TAPS[:k]), sum(TAPS[:k + 1])):
                            odd = tap % 2
                            now, of = padded[:, tap:tap + TOK], conv_acc[:, odd, :]
                            me.wait(last[odd])
                            if tap == 0:
                                ins = dve.tensor_scalar(of, now, taps_now[:, 0:1], taps_now[:, CONV_W:CONV_W + 1],
                                                        ALU.mult, ALU.add)
                            elif tap == 1:
                                ins = dve.tensor_scalar(of, now, taps_now[:, 1:2], None, ALU.mult)
                            else:
                                ins = dve.scalar_tensor_tensor(out=of, in0=now, scalar=taps_now[:, tap:tap + 1],
                                                               in1=of, op0=ALU.mult, op1=ALU.add)
                            me.step(ins)
                            last[odd] = me.n

            wide = z[:, CA0:CA0 + CT_T, :]

            def gated(g):
                dve.wait_ge(gate_sig, g + 1)
                for t in range(GT):
                    ga = z[:, GA0 + g * GT + t, :]
                    dve.wait_ge(bank_free, T_MERGE + g * GT + (t + 1 + GT))
                    dve.tensor_tensor(ga, val[t][:, :], ga, ALU.mult).then_inc(gated_ready, 1)

            for k in range(4 * U_H):
                if k and k % U_H == 0:
                    gated(k // U_H - 1)
                ahead(U_MERGE, k)
                if k == 0:
                    dve.wait_ge(conv_out, CT_T + 1)
                if 1 <= k <= U_D:
                    ada_unit(A_MERGE, k - 1)
                if k == 2:
                    dve.wait_ge(mean_sum, 1)
                    me.step(dve.tensor_scalar(usum[:, :], ps[4][:, :TOK], 1.0 / CONV_C, None, ALU.mult))
                    me.wait()
                    dve.tensor_tensor(wide, wide, usum[:, None, :].broadcast_to([P, CT_T, TOK]), ALU.subtract
                                      ).then_inc(centered, 1)
                if k == 7:
                    dve.wait_ge(croot, 1)
                    me.step(dve.reciprocal(rstd[:, :], rstd[:, :]))
                    me.wait()
                    dve.tensor_tensor(wide, wide, rstd[:, None, :].broadcast_to([P, CT_T, TOK]), ALU.mult
                                      ).then_inc(cnorm, 1)
                if k in (11, 12):
                    for t in range((k - 11) * 4, (k - 10) * 4):
                        dve.wait_ge(chi, t + 1)
                        dve.tensor_tensor(conv[:, t, 1, :], z[:, CA0 + t, :], conv[:, t, 0, :].bitcast(f32),
                                          ALU.subtract).then_inc(conv_ready, 1)
                if k == 13:
                    mod_out(13, 15 * GT)
                if k == 14:
                    me.step(dve.memset(acc_done, 0.0))
                    dve.wait_ge(centered, 1)
                    dve.memset(usum[:, :], 0.0).then_inc(zero_ready, 1)
            def merged(i, at):
                for t in range(GT):
                    tile = i * GT + (at * GT + t)
                    dve.wait_ge(bank_free, tile + (T_CONV + 1 + GT))
                    me.step(dve.tensor_tensor(val[t][:, :], val[t][:, :], z[:, tile + GC0, :], ALU.mult))
                me.wait()
                for t in range(GT):
                    tile = i * GT + (at * GT + t)
                    dve.tensor_tensor(val[t][:, :], val[t][:, :], z[:, tile + GA0, :], ALU.add).then_inc(m_val, 1)

            def merged_low(i, at):
                for t in range(GT):
                    tile = i * GT + (at * GT + t)
                    dve.wait_ge(m_hi, tile + 1)
                    dve.tensor_tensor(hs[:, tile, 1, :], val[t][:, :], hs[:, tile, 0, :].bitcast(f32),
                                      ALU.subtract).then_inc(m_ready, 1)

            def conv_group(i, at, first=False):
                for k in range(U_H):
                    if k == 0:
                        gated(3) if first else merged(i, at - 1)
                    if k == 2 and not first:
                        merged_low(i, at - 1)
                    ahead(U_CONV + at * U_H, k, i, U_H)
                    a = A_CONV + at * GT + k
                    dve.wait_ge(ada_here[k], i * 16 + (a // RING + 1) * 16)
                    dve.wait_ge(ada_free, i * 4 + (a + RING))
                    dve.scalar_tensor_tensor(
                        out=acc_done, in0=ada[k][:, 0, :], scalar=c_col[:, bass.ds(i * 4 + (at * 4 + k), 1)],
                        in1=acc_done, op0=ALU.mult, op1=ALU.add).then_inc(ada_free, 1)

            me.wait()
            conv_group(0, 0, True)
            dve.wait_ge(gate_sig, 8)
            dve.wait_ge(gated_ready, 4 * GT)
            for i in me.each(3, GT):
                conv_group(i, 1)

            def residual(i, at):
                for t in range(GT):
                    tile = i * GT + (at * GT + t)
                    xt = xT[:, tile, :]
                    dve.wait_ge(bank_free, tile + (T_MIX + 1 + GT))
                    dve.scalar_tensor_tensor(out=xt, in0=val[t][:, :], scalar=mod[:, bass.ds(tile + 2 * KT, 1)],
                                             in1=xt, op0=ALU.mult, op1=ALU.add).then_inc(x2_ready, 1)

            def mix(i, at):
                for k in range(U_D):
                    if k == 0:
                        residual(i, at - 1) if at else merged(0, 3)
                    if k == 2 and not at:
                        merged_low(0, 3)
                    if k == 3:
                        mod_out(i + (at + 14), i * GT + (at + 16) * GT)
                    if k == 5 and at == 3:
                        me.wait()
                        me.step(dve.scalar_tensor_tensor(out=gain[:, :], in0=mod[:, 4 * KT:5 * KT], scalar=1.0,
                                                         in1=g_ffn, op0=ALU.add, op1=ALU.mult))
                    if k == U_D - 1:
                        if at == 3:
                            residual(0, 3)
                    ahead(U_MIX + at * U_D, k, i, U_D)
                    if at < 3:
                        ada_unit(A_MIX + at * U_D, k, i)

            mix(0, 0)
            for i in me.each(2, U_D + 1):
                mix(i, 1)
            mix(0, 3)
            dve.wait_ge(root_ready, 2)
            dve.reciprocal(token_rms, token_rms).then_inc(token_ready, 1)
            dve.wait_ge(rms_wide, 1)
            for t in range(UK + 1):
                h_value(KT, t, ps[4][:, 0:TOK])
            h_split(KT, 0, 3 * KT)
            h_value(KT, UK + 1, ps[4][:, 0:TOK])
            h_split(KT, 1, 3 * KT)
            def gate_and_up(g, at, with_h=False):
                for n in range(2):
                    u, tile = U_FIN + (2 * at + n) * U_D, g * (2 * GT) + (T_FIN + (2 * at + n) * GT)
                    for k in range(U_D):
                        if with_h and n == 0 and k < U_D - 1:
                            for t in range(UK * (k + 1), UK * (k + 2)):
                                if t + UK < KT:
                                    h_value(KT, t + UK, ps[4][:, 0:TOK])
                                h_split(KT, t, 3 * KT)
                        ahead(u, k, g, 2 * U_D)
                    leave(tile, lambda t: (val, up)[n][t][:, :])
                for t in range(GT):
                    dve.wait_ge(g_silu, g * GT + (at * GT + t + 1))
                    dve.wait_ge(bank_free, tile + (t + 1 + GT))
                    dve.tensor_tensor(up[t][:, :], up[t][:, :], val[t][:, :], ALU.mult).then_inc(f_val, 1)
                for t in range(GT):
                    kt = g * GT + (at * GT + t)
                    dve.wait_ge(f_hi, kt + 1)
                    dve.tensor_tensor(hid[:, kt, 1, :], up[t][:, :], hid[:, kt, 0, :].bitcast(f32),
                                      ALU.subtract).then_inc(f_ready, 1)

            gate_and_up(0, 0, True)
            with dve.Fori(0, 10) as g:
                gate_and_up(g, 1)
            for g in range(4):
                for k in range(U_F):
                    ahead(U_FOUT + g * U_F, k)
                    if k < U_D:
                        ada_unit(A_FOUT + g * U_D, k, done=acc)
                    if k == 12:
                        mod_out(18 + g, (20 + g) * GT)
                tile = T_FOUT + g * GT
                leave(tile, lambda t: val[t][:, :])
                if g:
                    dve.wait_ge(o_t, g)
                me.wait()
                for t in range(GT):
                    col = 5 * KT + g * GT + t
                    dve.wait_ge(bank_free, tile + t + 1 + GT)
                    dve.scalar_tensor_tensor(out=out_t[:, t, :], in0=val[t][:, :], scalar=mod[:, col:col + 1],
                                             in1=xT[:, g * GT + t, :], op0=ALU.mult, op1=ALU.add
                                             ).then_inc(o_val, 1)

        @block.tensor
        def _(pe):
            def unit(first, k, of, tile, moving, i=0, per=0, ready=None, summed=False):
                n = first + k
                if ready:
                    pe.wait_ge(ready[0], ready[1] + UK * (k + 1))
                pe.wait_ge(w_split, i * per + (n + 1 + RING))
                for t in range(GT):
                    if k == 0:
                        pe.wait_ge(bank_free, tile + (t + 1))
                    for a in range(UK):
                        w = slice(t * P, (t + 1) * P)
                        both = moving(UK * k + a)
                        if summed:
                            pe.matmul(ps[t][:, :TOK], w_hi[n % RING][:, a, w], both[:, 0, :],
                                      start=(k == 0 and a == 0), stop=False)
                            pe.matmul(ps[t][:, :TOK], w_hi[n % RING][:, a, w], both[:, 1, :], start=False, stop=False)
                        else:
                            pe.matmul(ps[t][:, :], w_hi[n % RING][:, a, w], both, start=(k == 0 and a == 0),
                                      stop=False)
                        mm = pe.matmul(ps[t][:, :TOK], w_lo[n % RING][:, a, w], both[:, 0, :], start=False,
                                       stop=(k == of - 1 and a == UK - 1))
                    if k == of - 1 and t < GT - 1:
                        mm.then_inc(tile_done, 1)
                mm.then_inc(w_used, 1)

            def ada_sum(used, what, tiles=GT):
                pe.wait_ge(ada_free, used)
                for t in range(tiles):
                    mm = pe.matmul(ps[7][:, t:t + 1], what[:, t * P:(t + 1) * P], ones[:, 0:1], start=True, stop=True)
                mm.then_inc(mod_sum, 1)

            def h_tile(kt):
                return hs[:, kt, :, :]

            def attn_tile(kt):
                return attn[:, kt:kt + CB0 + 1:CB0, :]

            def conv_tile(kt):
                return conv[:, kt, :, :]

            def hid_tile(kt):
                return hid[:, kt, :, :]

            pe.wait_ge(small_here, SMALL * 16)
            pe.matmul(ps[6][0:HEADS, :P], rel[:, :], buckets[:, :], start=True, stop=True).then_inc(rows_t, 1)
            pe.wait_ge(x_here, 32)
            for b in range(KT // 2):
                if b >= 4:
                    pe.wait_ge(xsq_ready, b - 3)
                for t in range(2):
                    for r in range(2):
                        col = t * TOK + r * P
                        tr = pe.transpose(ps[b % 4][:, col:col + P], xtok[:, r, (2 * b + t) * P:(2 * b + t + 1) * P],
                                          ident)
                tr.then_inc(xt_done, 1)
            pe.wait_ge(cleared, CLEARS)
            for t in range(KT):
                if t % 2 == 0:
                    pe.wait_ge(xsq_ready, t // 2 + 1)
                mm = pe.matmul(ps[4][:, :TOK], ones[:, :], xsq[:, t, :], start=(t == 0), stop=(t == KT - 1))
            mm.then_inc(sum_ready, 1)
            pe.wait_ge(bias_here, 16)
            for b in range(HEADS // 2):
                if b >= 2:
                    pe.wait_ge(bias_out, b - 1)
                pe.matmul(ps[5 + b % 2][:, :], flip, reversed_bias[:, 2 * b:2 * b + 2, :], start=True, stop=True
                          ).then_inc(flipped, 1)
            with pe.Fori(0, 4) as g:
                ada_sum(g * U_D + (U_D + RING), wide_done, 2 * GT)
            def proj(g, first, norms):
                for k in range(U_D):
                    if k == 5:
                        ada_sum(g * U_D + (A_PROJ + first * U_D + RING), acc_done)
                    if norms and k == 3:
                        pe.wait_ge(norm_sq, g + 1)
                        for t in range(2):
                            for b in range(2):
                                mm = pe.matmul(ps[4][:, 4 * t + 2 * b:4 * t + 2 * b + 2], norm_in[:, t, b * P:(b + 1) * P],
                                               head_mean[:, 0:P:HEAD], start=True, stop=True)
                        mm.then_inc(norm_ms, 1)
                    if norms and k == 6:
                        pe.wait_ge(norm_rows, g + 1)
                        for t in range(2):
                            for b in range(2):
                                c = (2 * t + b) * P
                                mm = pe.matmul(ps[4][:, c:c + P], rms_rows[:, c:c + P], ident, start=True, stop=True)
                        mm.then_inc(norm_wide, 1)
                    unit(U_PROJ + first * U_D, k, U_D, g * GT + (T_PROJ + first * GT), h_tile, g, U_D,
                         (h_ready, 0) if first == 0 else None, summed=True)

            with pe.Fori(0, 2) as g:
                proj(g, 0, False)
            with pe.Fori(0, N_PROJ - 2) as g:
                proj(g, 2, True)
            for b in range(2):
                for t in range(2):
                    tr = pe.transpose(ps[6][:, (2 * b + t) * P:(2 * b + t + 1) * P], z[:, V0 + t, b * P:(b + 1) * P],
                                      ident)
            tr.then_inc(v_t, 1)
            pe.wait_ge(q_ready, 1)
            pe.matmul(ps[5][:, :], swap, z[:, K0:V0, :], start=True, stop=True).then_inc(swapped, 1)
            ada_sum(A_MERGE + RING, acc_done)
            with pe.Fori(0, N_GATE // 2) as m:
                for h in range(2):
                    n = m * 2 + (h + 1)
                    u, tile = U_GATE + h * U_D, m * (2 * GT) + (T_GATE + h * GT)
                    for k in range(U_D):
                        if k == 1:
                            pe.wait_ge(k_padded, 1)
                            pe.wait_ge(o_out, m * 2 + (h + 1))
                            pe.wait_ge(now_ready, m * 10 + (5 * h + 1))
                            for hd in range(2):
                                pe.matmul(ps[4 + hd][:, 0:P], q_now[:, 0:P], kz[:, hd, m, 0:P], start=True, stop=True)
                                mm = pe.matmul(ps[4 + hd][:, P:3 * P], q_now[:, P:2 * P], kz[:, hd, m, :], start=True,
                                               stop=True)
                            mm.then_inc(s_done, 1)
                        if k == 6:
                            pe.wait_ge(p_ready, n)
                            for hd in range(2):
                                for c in range(3):
                                    tr = pe.transpose(ps[6 + hd][:, c * P:(c + 1) * P], logit[:, hd, c * P:(c + 1) * P],
                                                      ident)
                            tr.then_inc(pt_done, 1)
                        if k == 7:
                            pe.wait_ge(pt_out, n * 2)
                            pe.wait_ge(now_ready, m * 10 + (5 * h + 5))
                            for b, parts in enumerate((((0, 0),), ((1, 0), (2, 1)))):
                                last = (1, parts[-1])
                                for hd in range(2):
                                    for c, keys in parts:
                                        v = v_now[:, keys, HEAD:3 * HEAD] if hd == 0 else v_now[:, keys, 0:2 * HEAD]
                                        mm = pe.matmul(ps[4][:, b * P:(b + 1) * P], v, probT[:, hd, c * P:(c + 1) * P],
                                                       start=(hd == 0 and (c, keys) == parts[0]),
                                                       stop=((hd, (c, keys)) == last))
                            mm.then_inc(o_done, 1)
                        unit(u, k, U_D, tile, h_tile, m, 2 * U_D, summed=True)

            for k in range(4 * U_H):
                if k == 2:
                    pe.wait_ge(conv_out, CT_T + 1)
                    pe.wait_ge(o_out, HEADS // 2 + 1)
                    for t in range(CT_T):
                        mm = pe.matmul(ps[4][:, :TOK], ones[:, :], z[:, CA0 + t, :], start=(t == 0),
                                       stop=(t == CT_T - 1))
                    mm.then_inc(mean_sum, 1)
                if k == 6:
                    pe.wait_ge(csq_ready, 1)
                    for t in range(CT_T):
                        mm = pe.matmul(ps[5][:, :TOK], ones[:, :], conv_sq[:, t, :], start=(t == 0),
                                       stop=(t == CT_T - 1))
                    mm.then_inc(var_sum, 1)
                if k == 12:
                    ada_sum(A_CONV + RING, acc_done)
                g, n = divmod(k, U_H)
                unit(U_MERGE + g * U_H, n, U_H, T_MERGE + g * GT, attn_tile,
                     ready=(o_out, 1) if k < 2 else None, summed=True)
            with pe.Fori(0, 4) as g:
                for k in range(U_H):
                    unit(U_CONV, k, U_H, g * GT + T_CONV, conv_tile, g, U_H, (conv_ready, 0),
                         summed=True)

            def token_squares(n, last=False):
                for t in range(GT):
                    pe.wait_ge(x2_sq, n + (t + 1))
                    for b in range(2):
                        mm = pe.matmul(ps[4][:, b:b + 1], val[t][:, b * P:(b + 1) * P], ones[:, 0:1], start=False,
                                       stop=(last and t == GT - 1 and b == 1))
                mm.then_inc(sq_summed, 1)

            def mix(i, at):
                for k in range(U_D):
                    if k == 2:
                        ada_sum(i * U_D + (A_MIX + at * U_D + RING), acc_done)
                    if k == 3 and at:
                        token_squares(i * GT + (at - 1) * GT)
                    unit(U_MIX + at * U_D, k, U_D, i * GT + (T_MIX + at * GT), h_tile, i, U_D,
                         (m_ready, 0), summed=True)

            pe.wait_ge(zero_ready, 1)
            pe.matmul(ps[4][:, 0:2], usum[:, 0:P], ones[:, 0:2], start=True, stop=False)
            mix(0, 0)
            with pe.Fori(0, 2) as i:
                mix(i, 1)
            mix(0, 3)
            token_squares(3 * GT, True)
            pe.wait_ge(token_ready, 1)
            for b in range(2):
                mm = pe.matmul(ps[4][:, b * P:(b + 1) * P], token_rms[:, b:b + 1].broadcast_to([P, P]), ident,
                               start=True, stop=True)
            mm.then_inc(rms_wide, 1)
            with pe.Fori(0, 11) as g:
                for n in range(2):
                    for k in range(U_D):
                        unit(U_FIN + n * U_D, k, U_D, g * (2 * GT) + (T_FIN + n * GT), h_tile, g, 2 * U_D,
                             (h_ready, KT) if n == 0 else None)

            def to_rows(n):
                pe.wait_ge(o_val, n)
                for b in range(2):
                    for t in range(GT):
                        tr = pe.transpose(ps[4 + b][:, t * P:(t + 1) * P], out_t[:, t, b * P:(b + 1) * P], ident)
                tr.then_inc(o_t, 1)

            with pe.Fori(0, 2) as m:
                for h in range(2):
                    for k in range(U_F):
                        if k == 11:
                            ada_sum(m * (2 * U_D) + (A_FOUT + (h + 1) * U_D + RING), acc)
                        if k == 5 and h == 1:
                            to_rows(m * (2 * GT) + GT)
                        unit(U_FOUT + h * U_F, k, U_F, m * (2 * GT) + (T_FOUT + h * GT), hid_tile, m, 2 * U_F,
                             (f_ready, 0) if h == 0 else None)
                to_rows(m * (2 * GT) + 2 * GT)


def kernel(x, c, w_ada, b_ada, norm_mix_g, w_in, q_norm_g, k_norm_g, attn_sinks, rel_bias, w_attn_out,
           conv_w, conv_b, conv_ln_g, conv_ln_b, w_conv_out, w_mix_out, norm_ffn_g, w_ffn_in, w_ffn_out):
    import math

    import numpy as np
    import concourse.bacc as bacc
    from concourse.bass_utils import run_bass_kernel_spmd

    p = np.arange(P)
    squares = np.zeros((P, 4, P), np.float32)
    squares[p, 0, p] = 1
    squares[p, 1, P - 1 - p] = 1
    squares[p, 2, (p + HEAD) % P] = 1
    squares[:, 3, :] = (p[:, None] // HEAD == p[None, :] // HEAD) / HEAD
    onehot = np.zeros((32, P), np.float32)
    for j in range(P):
        dist = P - 1 - j
        bucket = dist if dist < 16 else min(31, 16 + int(math.log(dist / 16) / math.log(P / 16) * 16))
        onehot[bucket, j] = 1

    parts = (c, b_ada, norm_mix_g, norm_ffn_g, conv_ln_g, conv_ln_b)
    vectors = np.concatenate([np.asarray(v).reshape(-1, P).T for v in parts], axis=1)
    taps = np.concatenate([conv_w[0], conv_b.reshape(1, CONV_C)]).reshape(CONV_W + 1, CT_T, P).transpose(2, 1, 0)

    arrays = {
        "x": x[0], "w_ada": w_ada[0], "w_in": w_in[0], "vectors": vectors, "taps": taps,
        "q_norm_g": q_norm_g.reshape(HEAD, 1), "k_norm_g": k_norm_g.reshape(HEAD, 1),
        "attn_sinks": attn_sinks.reshape(1, HEADS), "rel_bias": rel_bias, "w_attn_out": w_attn_out[0],
        "w_conv_out": w_conv_out[0], "w_mix_out": w_mix_out[0], "w_ffn_in": w_ffn_in[0],
        "w_ffn_out": w_ffn_out[0],
        "squares": squares, "onehot": onehot,
    }
    arrays = {name: np.ascontiguousarray(a) for name, a in arrays.items()}
    nc = bacc.Bacc("TRN2", target_bir_lowering=False, num_devices=1, dynamic_dma_scratch_size=1024)
    args = {name: nc.dram_tensor(f"in_{name}", a.shape, mybir.dt.from_np(a.dtype), kind="ExternalInput").ap()
            for name, a in arrays.items()}
    out = nc.dram_tensor("out", (TOK, D), f32, kind="ExternalOutput").ap()
    build(nc, *args.values(), out)
    result = run_bass_kernel_spmd(nc, [{f"in_{name}": a for name, a in arrays.items()}], core_ids=[0])
    return result.results[0]["out"].reshape(1, TOK, D)
```
